# Optimizing a Trainium2 kernel written in Bass

```python
import jax
import jax.numpy as jnp
from jax import lax
import numpy as np

D_MODEL = 1024
BATCH = 1
SEQ = 2048
DEPTH = 1

EPS = 1e-6
N_MEM = 256
D_MIX = D_MODEL
POOL_WIDTH = D_MIX // 2
POOL_GROUPS = 4
POOL_GROUP_DIM = POOL_WIDTH // POOL_GROUPS
POOL_WINDOWS = (2, 4, 8, 16)
MLSTM_WIDTH = D_MIX - POOL_WIDTH
MLSTM_HEADS = 4
MLSTM_HEAD_DIM = MLSTM_WIDTH // MLSTM_HEADS
CONV_WIDTH = 4
CHUNK = 64
XATTN_HEADS = 4
XATTN_HEAD_DIM = D_MODEL // XATTN_HEADS
D_FF = -(-8 * D_MODEL // (3 * 256)) * 256

OFF_Q = POOL_WIDTH
OFF_K = OFF_Q + MLSTM_WIDTH
OFF_V = OFF_K + MLSTM_WIDTH
OFF_O = OFF_V + MLSTM_WIDTH
OFF_GATE = OFF_O + MLSTM_WIDTH
IN_COLS = OFF_GATE + 2 * MLSTM_HEADS

kernel_name = "hybrid_pool_mlstm_memxattn_block"

def rmsnorm(x, g):
    xf = x.astype(jnp.float32)
    y = xf * lax.rsqrt(jnp.mean(xf * xf, axis=-1, keepdims=True) + EPS)
    return (y * g.astype(jnp.float32)).astype(x.dtype)

def causal_depthwise_conv(x, w):
    C = x.shape[-1]
    return lax.conv_general_dilated(
        x, w[:, None, :].astype(x.dtype), window_strides=(1,),
        padding=[(CONV_WIDTH - 1, 0)], dimension_numbers=('NWC', 'WIO', 'NWC'),
        feature_group_count=C)

def pool_mixer(u, w_pool, scale):
    B, S, _ = u.shape
    uf = u.astype(jnp.float32).reshape(B, S, POOL_GROUPS, POOL_GROUP_DIM)
    cs = jnp.concatenate([jnp.zeros_like(uf[:, :1]), jnp.cumsum(uf, axis=1)], axis=1)
    t = jnp.arange(S)[:, None]
    win = jnp.asarray(POOL_WINDOWS, dtype=jnp.int32)[None, :]
    start = jnp.maximum(t + 1 - win, 0)
    count = (t + 1 - start).astype(jnp.float32)
    window_sum = cs[:, 1:] - cs[:, start, jnp.arange(POOL_GROUPS)[None, :], :]
    d = window_sum / count[None, :, :, None] - uf
    y = jnp.einsum('bsgc,gcd->bsgd', d, w_pool.astype(jnp.float32))
    return (y.reshape(B, S, POOL_WIDTH) * scale.astype(jnp.float32)).astype(u.dtype)

def _chunk_seq(t):
    B, H, S = t.shape[:3]
    t = t.reshape((B, H, S // CHUNK, CHUNK) + t.shape[3:])
    return jnp.moveaxis(t, 2, 0)

def mlstm_heads(q, k, v, i_pre, f_pre):
    B, S, H, dh = q.shape
    q = q * dh ** -0.5
    qc, kc, vc = (_chunk_seq(jnp.swapaxes(t, 1, 2)) for t in (q, k, v))
    ic = _chunk_seq(jnp.swapaxes(i_pre, 1, 2))
    fc = _chunk_seq(jnp.swapaxes(jax.nn.log_sigmoid(f_pre), 1, 2))
    tril = jnp.tril(jnp.ones((CHUNK, CHUNK), dtype=bool))

    def step(carry, inp):
        C, n, m = carry
        qb, kb, vb, ib, fb = inp
        b = jnp.cumsum(fb, axis=-1)
        D = jnp.where(tril, b[..., :, None] - b[..., None, :] + ib[..., None, :], -jnp.inf)
        inter = b + m[..., None]
        m_i = jnp.maximum(jnp.max(D, axis=-1), inter)
        A = jnp.einsum('bhid,bhjd->bhij', qb, kb) * jnp.exp(D - m_i[..., None])
        w_inter = jnp.exp(inter - m_i)
        num = jnp.einsum('bhij,bhjd->bhid', A, vb) + w_inter[..., None] * jnp.einsum('bhid,bhde->bhie', qb, C)
        den = jnp.sum(A, axis=-1) + w_inter * jnp.einsum('bhid,bhd->bhi', qb, n)
        h = num / jnp.maximum(jnp.abs(den), jnp.exp(-m_i))[..., None]
        bL = b[..., -1]
        g = bL[..., None] - b + ib
        m_new = jnp.maximum(bL + m, jnp.max(g, axis=-1))
        decay = jnp.exp(bL + m - m_new)
        wk = jnp.exp(g - m_new[..., None])
        C_new = decay[..., None, None] * C + jnp.einsum('bhj,bhjd,bhje->bhde', wk, kb, vb)
        n_new = decay[..., None] * n + jnp.einsum('bhj,bhjd->bhd', wk, kb)
        return (C_new, n_new, m_new), h

    init = (jnp.zeros((B, H, dh, dh), jnp.float32), jnp.zeros((B, H, dh), jnp.float32),
            jnp.zeros((B, H), jnp.float32))
    _, h = lax.scan(step, init, (qc, kc, vc, ic, fc))
    h = jnp.moveaxis(h, 0, 2).reshape(B, H, S, dh)
    return jnp.swapaxes(h, 1, 2)

def cross_attention(xn, mem_n, wq, wk, wv, wo):
    B, S, _ = xn.shape
    M = mem_n.shape[1]
    q = (xn @ wq).reshape(B, S, XATTN_HEADS, XATTN_HEAD_DIM).astype(jnp.float32)
    k = (mem_n @ wk).reshape(B, M, XATTN_HEADS, XATTN_HEAD_DIM).astype(jnp.float32)
    v = (mem_n @ wv).reshape(B, M, XATTN_HEADS, XATTN_HEAD_DIM).astype(jnp.float32)
    p = jax.nn.softmax(jnp.einsum('bshd,bmhd->bhsm', q, k) * XATTN_HEAD_DIM ** -0.5, axis=-1)
    o = jnp.einsum('bhsm,bmhd->bshd', p, v).reshape(B, S, D_MODEL).astype(xn.dtype)
    return o @ wo

def swiglu(xn, wg, wu, wd):
    return (jax.nn.silu(xn @ wg) * (xn @ wu)) @ wd

def setup_inputs(seed: int = 0) -> dict:
    key = jax.random.key(seed)
    ks = jax.random.split(key, 24)

    def nrm(k, shape, scale):
        return jax.random.normal(k, shape, jnp.float32) * scale

    def gain(k, shape):
        return 1.0 + 0.02 * jax.random.normal(k, shape, jnp.float32)

    H = MLSTM_HEADS
    b_i = nrm(ks[3], (DEPTH, H), 0.1)
    b_f = jnp.linspace(3.0, 6.0, H, dtype=jnp.float32)[None, :] + nrm(ks[4], (DEPTH, H), 0.1)
    return {
        'x': nrm(ks[0], (BATCH, SEQ, D_MODEL), 1.0),
        'mem': nrm(ks[1], (BATCH, N_MEM, D_MODEL), 1.0),
        'w_in': nrm(ks[2], (DEPTH, D_MODEL, IN_COLS), D_MODEL ** -0.5),
        'b_gate': jnp.concatenate([b_i, b_f], axis=-1),
        'conv_qk': nrm(ks[5], (DEPTH, CONV_WIDTH, 2 * MLSTM_WIDTH), CONV_WIDTH ** -0.5),
        'w_pool': nrm(ks[6], (DEPTH, POOL_GROUPS, POOL_GROUP_DIM, POOL_GROUP_DIM), POOL_GROUP_DIM ** -0.5),
        'pool_scale': gain(ks[7], (DEPTH, POOL_WIDTH)),
        'mlstm_norm_g': gain(ks[8], (DEPTH, MLSTM_WIDTH)),
        'w_out': nrm(ks[9], (DEPTH, D_MIX, D_MODEL), D_MIX ** -0.5),
        'g_mix_pre': gain(ks[10], (DEPTH, D_MODEL)),
        'g_mix_post': gain(ks[11], (DEPTH, D_MODEL)),
        'g_mem': gain(ks[12], (DEPTH, D_MODEL)),
        'g_xattn_pre': gain(ks[13], (DEPTH, D_MODEL)),
        'g_xattn_post': gain(ks[14], (DEPTH, D_MODEL)),
        'wq_x': nrm(ks[15], (DEPTH, D_MODEL, D_MODEL), D_MODEL ** -0.5),
        'wk_x': nrm(ks[16], (DEPTH, D_MODEL, D_MODEL), D_MODEL ** -0.5),
        'wv_x': nrm(ks[17], (DEPTH, D_MODEL, D_MODEL), D_MODEL ** -0.5),
        'wo_x': nrm(ks[18], (DEPTH, D_MODEL, D_MODEL), D_MODEL ** -0.5),
        'g_ffn_pre': gain(ks[19], (DEPTH, D_MODEL)),
        'g_ffn_post': gain(ks[20], (DEPTH, D_MODEL)),
        'w_gate': nrm(ks[21], (DEPTH, D_MODEL, D_FF), D_MODEL ** -0.5),
        'w_up': nrm(ks[22], (DEPTH, D_MODEL, D_FF), D_MODEL ** -0.5),
        'w_down': nrm(ks[23], (DEPTH, D_FF, D_MODEL), D_FF ** -0.5),
    }

def reference(x, mem, w_in, b_gate, conv_qk, w_pool, pool_scale, mlstm_norm_g, w_out,
              g_mix_pre, g_mix_post, g_mem, g_xattn_pre, g_xattn_post,
              wq_x, wk_x, wv_x, wo_x, g_ffn_pre, g_ffn_post, w_gate, w_up, w_down):
    B, S, _ = x.shape
    H, dh = MLSTM_HEADS, MLSTM_HEAD_DIM
    for l in range(DEPTH):
        h = rmsnorm(x, g_mix_pre[l])
        proj = h @ w_in[l]
        pool_out = pool_mixer(proj[..., :OFF_Q], w_pool[l], pool_scale[l])
        qk = jax.nn.silu(causal_depthwise_conv(proj[..., OFF_Q:OFF_V], conv_qk[l])).astype(jnp.float32)
        q = qk[..., :MLSTM_WIDTH].reshape(B, S, H, dh)
        k = qk[..., MLSTM_WIDTH:].reshape(B, S, H, dh)
        v = proj[..., OFF_V:OFF_O].astype(jnp.float32).reshape(B, S, H, dh)
        o_gate = jax.nn.sigmoid(proj[..., OFF_O:OFF_GATE].astype(jnp.float32))
        gates = proj[..., OFF_GATE:].astype(jnp.float32) + b_gate[l].astype(jnp.float32)
        hm = mlstm_heads(q, k, v, gates[..., :H], gates[..., H:])
        hm = hm * lax.rsqrt(jnp.mean(hm * hm, axis=-1, keepdims=True) + EPS)
        m_out = (hm.reshape(B, S, MLSTM_WIDTH) * mlstm_norm_g[l].astype(jnp.float32) * o_gate).astype(x.dtype)
        mix = jnp.concatenate([pool_out, m_out], axis=-1) @ w_out[l]
        x = x + rmsnorm(mix, g_mix_post[l])
        h = rmsnorm(x, g_xattn_pre[l])
        mem_n = rmsnorm(mem, g_mem[l])
        x = x + rmsnorm(cross_attention(h, mem_n, wq_x[l], wk_x[l], wv_x[l], wo_x[l]), g_xattn_post[l])
        h = rmsnorm(x, g_ffn_pre[l])
        x = x + rmsnorm(swiglu(h, w_gate[l], w_up[l], w_down[l]), g_ffn_post[l])
    return x


_drawn_inputs = setup_inputs


def setup_inputs(seed=0):
    import zlib

    import numpy as np

    out = dict(_drawn_inputs(seed))
    spreads = {}
    factors = {'pool_scale': 4.177,
     'mlstm_norm_g': 6.995,
     'g_mix_pre': 2.908,
     'g_mix_post': 3.572,
     'g_mem': 2.99,
     'g_xattn_pre': 4.196,
     'g_xattn_post': 13.46,
     'g_ffn_pre': 10.877,
     'g_ffn_post': 24.427}
    for name, (base, spread) in spreads.items():
        noise = np.random.default_rng([zlib.crc32(name.encode()), seed]).standard_normal(out[name].shape)
        drawn = base * np.exp(spread * noise) if base else spread * noise
        out[name] = jnp.asarray(drawn.astype(out[name].dtype))
    for name, factor in factors.items():
        out[name] = (out[name] * factor).astype(out[name].dtype)
    return out
```

```python
from contextlib import ExitStack

import concourse.bass as bass
from concourse import mybir

F32 = mybir.dt.float32
FR = mybir.dt.float32r
ACT = mybir.ActivationFunctionType
ALU = mybir.AluOpType
AX_X = mybir.AxisListType.X

P = 128
SEQ = 2048
D = 1024
KT = D // P
NT = SEQ // P
EPS = 1e-6
N_MEM = 256
HEADS = 4
DH = 128
X_DH = 256
POOL_WINDOWS = (2, 4, 8, 16)
D_FF = 2816
BANK = 512
NQ = SEQ // BANK
HC = HEADS * NT
PANELS = 21
HALO = 16
LOW = -1e30
LOG_EXP = "natural_log_exp_and_others"


class Scope(ExitStack):

    def __init__(self, nc, tag):
        super().__init__()
        self.nc, self.tag = nc, tag

    def sb(self, name, shape, dt=F32):
        return self.enter_context(self.nc.sbuf_tensor(f"{self.tag}_{name}", shape, dt))

    def ps(self, name, shape, dt=F32):
        return self.enter_context(self.nc.psum_tensor(f"{self.tag}_{name}", shape, dt))

    def sem(self, name):
        return self.enter_context(self.nc.semaphore(f"{self.tag}_{name}"))

    def sems(self, name, n):
        return [self.sem(f"{name}{i}") for i in range(n)]


class Order:

    def __init__(self, eng, sem):
        self.eng, self.sem, self.base, self.n = eng, sem, 0, 0

    def after(self, ins):
        self.n += 1
        ins.then_inc(self.sem, 1)
        self.eng.wait_ge(self.sem, self.base + self.n)

    def start(self, i, per):
        self.kept = self.base + self.n
        self.base, self.n, self.per = self.kept + i * per, 0, per

    def end(self, turns):
        assert self.n == self.per, (self.n, self.per)
        self.base, self.n = self.kept + turns * self.per, 0


def at_least(eng, sem, n):
    if not isinstance(n, int) or n > 0:
        eng.wait_ge(sem, n)


def rows_all(vector):
    return vector.partition_broadcast(P)


def rsqrt_start(nc, order, y0, ss, scale, eps):
    order.after(nc.scalar.activation(y0, ss, ACT.Ln, scale=scale, bias=eps))
    return nc.scalar.activation(y0, y0, ACT.Exp, scale=-0.5)


def rsqrt_end(nc, order, out, y0, ss, tmp, scale, eps):
    order.after(nc.vector.tensor_scalar(tmp, ss, scale, eps, ALU.mult, ALU.add))
    order.after(nc.vector.tensor_tensor(tmp, tmp, y0, ALU.mult))
    order.after(nc.vector.tensor_tensor(tmp, tmp, y0, ALU.mult))
    order.after(nc.vector.tensor_scalar(tmp, tmp, -0.5, 1.5, ALU.mult, ALU.add))
    return nc.vector.tensor_tensor(out, tmp, y0, ALU.mult)


def make_identity(nc, g, sem, ident):
    g.memset(ident[:], 0.0).then_inc(sem, 1)
    g.wait_ge(sem, 1)
    g.affine_select(out=ident[:], in_=ident[:], compare_op=ALU.not_equal, fill=1.0, base=0,
                    pattern=[[-1, P]], channel_multiplier=1).then_inc(sem, 1)
    g.wait_ge(sem, 2)


def memory_side(nc, t, ident):
    with Scope(nc, "ms") as c:
        mem = c.sb("mem", [P, 2, D])
        mem_n = c.sb("mem_n", [P, 2, D])
        mem_t = c.sb("mem_t", [P, KT, N_MEM])
        wk, wv, wqt, wo = (c.sb(n, [P, KT, D]) for n in ("wk", "wv", "wqt", "wo"))
        w_out = c.sb("w_out", [P, 4, D])
        pool_t = c.sb("pool_t", [P, 4, P])
        g_mem, g_q = c.sb("g_mem", [P, KT]), c.sb("g_q", [P, KT])
        pool_s = c.sb("pool_s", [P, 4])
        k_t, v_t = c.sb("k_t", [P, KT, N_MEM]), c.sb("v_t", [P, KT, N_MEM])
        STAGES = 2
        stage = c.sb("stage", [P, STAGES, D])
        ss, y0, tmp, rs = (c.sb(n, [P, 2]) for n in ("ss", "y0", "tmp", "rs"))
        acc = c.ps("acc", [P, 4, BANK])
        tr = c.ps("tr", [P, 4, BANK])
        ld_mem, ld_small = c.sem("ld_mem"), c.sem("ld_small")
        ld = dict((n, c.sem("ld_" + n)) for n in ("wk", "wv", "wqt", "wo", "w_out"))
        act_own, dve_own = c.sem("act_own"), c.sem("dve_own")
        ident_made, guess, mem_normed, mem_turned = (
            c.sem(n) for n in ("ident_made", "guess", "mem_normed", "mem_turned"))
        mem_t_ready, consts_ready, product, evacuated = (
            c.sem(n) for n in ("mem_t_ready", "consts_ready", "product", "evacuated"))
        stored = c.sems("stored", STAGES)
        block = c.enter_context(nc.Block())

        rows = ([("a", r) for r in range(KT)] + [("b", r) for r in range(KT)] +
                [("pool", r) for r in range(4)])
        FIRST_ROW = 8
        dest = {"a": t["a_mat"], "b": t["b_mat"], "pool": t["pool_out"]}

        @block.gpsimd
        def _(g):
            make_identity(nc, g, ident_made, ident)

        @block.sync
        def _(sp):
            sp.dma_start(mem[:], t["mem"].rearrange("(a p) d -> p a d", p=P)).then_inc(ld_mem, 16)
            sp.dma_start(g_mem[:], t["g_mem_cols"]).then_inc(ld_small, 16)
            sp.dma_start(g_q[:], t["g_xattn_pre_cols"]).then_inc(ld_small, 16)
            sp.dma_start(pool_s[:], t["pool_scale_cols"]).then_inc(ld_small, 16)
            sp.dma_start(pool_t[:], t["w_pool_t"].rearrange("g d c -> d g c")).then_inc(ld_small, 16)
            for name, to in (("wk", wk), ("wv", wv), ("wqt", wqt), ("wo", wo)):
                sp.dma_start(to[:], t[name].rearrange("(k p) n -> p k n", p=P)).then_inc(ld[name], 16)
            sp.dma_start(w_out[:], t["w_out"][0:4 * P].rearrange("(k p) n -> p k n", p=P)).then_inc(ld["w_out"], 16)
            for r, (kind, at) in enumerate(rows):
                sp.wait_ge(evacuated, FIRST_ROW + 2 * r + 2)
                sp.dma_start(dest[kind][at * P:(at + 1) * P], stage[:, r % STAGES]).then_inc(stored[r % STAGES], 16)
            for s in range(STAGES):
                sp.wait_ge(stored[s], 16 * len(range(s, len(rows), STAGES)))

        @block.scalar
        def _(act):
            own = Order(act, act_own)
            act.preload_act_table_set(LOG_EXP)
            act.wait_ge(ld_mem, 16)
            for i in range(2):
                own.after(nc.scalar.activation(mem_n[:, i], mem[:, i], ACT.Square, accum_out=ss[:, i:i + 1]))
            rsqrt_start(nc, own, y0[:], ss[:], 1.0 / D, EPS).then_inc(guess, 1)
            act.wait_ge(ld_small, 64)
            for k in range(KT):
                act.wait_ge(mem_turned, k // 2 + 1)
                nc.scalar.activation(mem_t[:, k], tr[:, k // 2, (k % 2) * N_MEM:(k % 2 + 1) * N_MEM], ACT.Copy,
                                     scale=g_mem[:, k:k + 1]).then_inc(mem_t_ready, 1)
            act.wait_ge(consts_ready, 2)
            for j in range(8):
                act.wait_ge(product, j + 1)
                to = (k_t if j < 4 else v_t)[:, 2 * (j % 4):2 * (j % 4) + 2]
                nc.scalar.activation(to, acc[:, j % 4].rearrange("p (a m) -> p a m", a=2), ACT.Copy).then_inc(evacuated, 1)
            for r, (kind, at) in enumerate(rows):
                for half in range(2):
                    j = FIRST_ROW + 2 * r + half
                    act.wait_ge(product, j + 1)
                    if r >= STAGES:
                        act.wait_ge(stored[r % STAGES], 16 * (r // STAGES))
                    scale = g_q[:, at:at + 1] if kind == "a" else 1.0
                    nc.scalar.activation(stage[:, r % STAGES, half * BANK:(half + 1) * BANK], acc[:, j % 4],
                                         ACT.Copy, scale=scale).then_inc(evacuated, 1)

        @block.vector
        def _(dve):
            own = Order(dve, dve_own)
            dve.wait_ge(ld_small, 64)
            nc.vector.tensor_scalar(g_q[:], g_q[:], X_DH ** -0.5, None, ALU.mult).then_inc(consts_ready, 1)
            nc.vector.tensor_tensor(pool_t[:], pool_t[:], pool_s[:].unsqueeze(2).to_broadcast([P, 4, P]),
                                    ALU.mult).then_inc(consts_ready, 1)
            dve.wait_ge(guess, 1)
            own.after(rsqrt_end(nc, own, rs[:], y0[:], ss[:], tmp[:], 1.0 / D, EPS))
            for i in range(2):
                nc.vector.tensor_scalar(mem_n[:, i], mem[:, i], rs[:, i:i + 1], None, ALU.mult).then_inc(mem_normed, 1)

        @block.tensor
        def _(pe):
            pe.wait_ge(ident_made, 2)
            pe.wait_ge(mem_normed, 2)
            for k in range(KT):
                for i in range(2):
                    at = (k % 2) * N_MEM + i * P
                    last = nc.tensor.transpose(tr[:, k // 2, at:at + P], mem_n[:, i, k * P:(k + 1) * P], ident[:])
                if k % 2:
                    last.then_inc(mem_turned, 1)
            pe.wait_ge(mem_t_ready, KT)
            for j in range(8):
                pe.wait_ge(ld["wk" if j < 4 else "wv"], 16)
                if j >= 4:
                    pe.wait_ge(evacuated, j - 3)
                w = wk if j < 4 else wv
                for a in range(2):
                    d = 2 * (j % 4) + a
                    for k in range(KT):
                        last = nc.tensor.matmul(acc[:, j % 4, a * N_MEM:(a + 1) * N_MEM], w[:, k, d * P:(d + 1) * P],
                                                mem_t[:, k], start=(k == 0), stop=(k == KT - 1))
                last.then_inc(product, 1)
            for name in ("wqt", "wo", "w_out"):
                pe.wait_ge(ld[name], 16)
            pe.wait_ge(consts_ready, 2)
            pe.wait_ge(evacuated, 8)
            for r, (kind, at) in enumerate(rows):
                for half in range(2):
                    j = FIRST_ROW + 2 * r + half
                    pe.wait_ge(evacuated, j - 3)
                    if kind == "a":
                        for a in range(2):
                            head = 2 * half + a
                            for dd in range(2):
                                last = nc.tensor.matmul(acc[:, j % 4, a * N_MEM:(a + 1) * N_MEM],
                                                        wqt[:, 2 * head + dd, at * P:(at + 1) * P],
                                                        k_t[:, 2 * head + dd], start=(dd == 0), stop=(dd == 1))
                    elif kind == "b":
                        head, mm = divmod(at, 2)
                        for dd in range(2):
                            last = nc.tensor.matmul(acc[:, j % 4], v_t[:, 2 * head + dd, mm * P:(mm + 1) * P],
                                                    wo[:, 2 * head + dd, half * BANK:(half + 1) * BANK],
                                                    start=(dd == 0), stop=(dd == 1))
                    else:
                        last = nc.tensor.matmul(acc[:, j % 4], pool_t[:, at], w_out[:, at, half * BANK:(half + 1) * BANK],
                                                start=True, stop=True)
                    last.then_inc(product, 1)


def mix_pre(nc, t, ident, h_hi, h_lo):
    with Scope(nc, "mp") as c:
        gain = c.sb("gain", [P, D])
        x = c.sb("x", [P, 2, D])
        h = c.sb("h", [P, 2, D])
        junk = c.sb("junk", [P, D])
        ss, y0, tmp, rs = (c.sb(n, [P, 2]) for n in ("ss", "y0", "tmp", "rs"))
        tr = c.ps("tr", [P, 2, KT, P])
        ld_gain, ld_x = c.sem("ld_gain"), c.sems("ld_x", 2)
        act_own, dve_own = c.sem("act_own"), c.sem("dve_own")
        guess, h_ready, turned, hi_ready, lo_ready = (
            c.sem(n) for n in ("guess", "h_ready", "turned", "hi_ready", "lo_ready"))
        block = c.enter_context(nc.Block())
        x_d = t["x"].rearrange("(t p) d -> t p d", p=P)

        @block.sync
        def _(sp):
            sp.dma_start(gain[:], rows_all(t["g_mix_pre"])).then_inc(ld_gain, 16)
            for s in range(2):
                sp.dma_start(x[:, s], x_d[s]).then_inc(ld_x[s], 16)
            with sp.Fori(1, NT // 2) as i:
                for s in range(2):
                    sp.wait_ge(h_ready, 2 * i + s - 1)
                    sp.dma_start(x[:, s], x_d[2 * i + s]).then_inc(ld_x[s], 16)

        @block.scalar
        def _(act):
            own = Order(act, act_own)
            act.preload_act_table_set(LOG_EXP)

            def stats(i, s):
                act.wait_ge(ld_x[s], 16 * (i + 1))
                own.after(nc.scalar.activation(junk[:], x[:, s], ACT.Square, accum_out=ss[:, s:s + 1]))
                rsqrt_start(nc, own, y0[:, s:s + 1], ss[:, s:s + 1], 1.0 / D, EPS).then_inc(guess, 1)

            def high(tile, s):
                act.wait_ge(turned, tile + 1)
                nc.scalar.activation(h_hi[:, :, bass.ds(tile * P, P)], tr[:, s], ACT.Copy).then_inc(hi_ready, 1)

            own.start(0, 2)
            stats(0, 0)
            own.end(1)
            own.start(0, 2)
            stats(0, 1)
            own.end(1)
            high(0, 0)
            with act.Fori(1, NT // 2) as i:
                own.start(i - 1, 4)
                stats(i, 0)
                high(2 * i - 1, 1)
                stats(i, 1)
                high(2 * i, 0)
            own.end(NT // 2 - 1)
            high(NT - 1, 1)

        @block.vector
        def _(dve):
            own = Order(dve, dve_own)

            def normalise(tile, s, first=False):
                dve.wait_ge(guess, tile + 1)
                if not first:
                    dve.wait_ge(turned, tile - 1)
                own.after(rsqrt_end(nc, own, rs[:, s:s + 1], y0[:, s:s + 1], ss[:, s:s + 1], tmp[:, s:s + 1],
                                    1.0 / D, EPS))
                nc.vector.scalar_tensor_tensor(h[:, s], x[:, s], rs[:, s:s + 1], gain[:], ALU.mult,
                                               ALU.mult).then_inc(h_ready, 1)

            def low(tile, s):
                dve.wait_ge(hi_ready, tile + 1)
                at = bass.ds(tile * P, P)
                nc.vector.tensor_tensor(h_lo[:, :, at], tr[:, s], h_hi[:, :, at].bitcast(F32),
                                        ALU.subtract).then_inc(lo_ready, 1)

            dve.wait_ge(ld_gain, 16)
            normalise(0, 0, True)
            normalise(1, 1, True)
            low(0, 0)
            with dve.Fori(1, NT // 2) as i:
                own.start(i - 1, 10)
                normalise(2 * i, 0)
                low(2 * i - 1, 1)
                normalise(2 * i + 1, 1)
                low(2 * i, 0)
            own.end(NT // 2 - 1)
            low(NT - 1, 1)

        @block.tensor
        def _(pe):
            def turn(tile, s, first=False):
                pe.wait_ge(h_ready, tile + 1)
                if not first:
                    pe.wait_ge(lo_ready, tile - 1)
                for k in range(KT):
                    last = nc.tensor.transpose(tr[:, s, k], h[:, s, k * P:(k + 1) * P], ident[:])
                last.then_inc(turned, 1)

            turn(0, 0, True)
            turn(1, 1, True)
            with pe.Fori(1, NT // 2) as i:
                turn(2 * i, 0)
                turn(2 * i + 1, 1)


def mix_in(nc, t, h_hi, h_lo, gate_rows):
    with Scope(nc, "mi") as c:
        raw = c.sb("raw", [P, 2, KT, P])
        w_hi, w_lo = c.sb("w_hi", [P, 2, KT, P], FR), c.sb("w_lo", [P, 2, KT, P], FR)
        u = c.sb("u", [P, 2, HALO + SEQ])
        wa, wb = c.sb("wa", [P, HALO + SEQ]), c.sb("wb", [P, HALO + SEQ])
        res = c.sb("res", [P, 2, SEQ])
        taps = c.sb("taps", [P, KT, 4])
        bias = c.sb("bias", [P, 1])
        inv = c.sb("inv", [P, HALO])
        edge = c.sb("edge", [P, HALO])
        ga, gb, gi = gate_rows
        gf, gm, one = (c.sb(n, [HC, P]) for n in ("gf", "gm", "one"))
        ends = c.sb("ends", [HC, 2])
        heads = c.sb("heads", [HEADS, NT, 2])
        prev = c.sb("prev", [HEADS, NT + 1])
        m_prev = c.sb("m_prev", [HC, 1])
        acc = c.ps("acc", [P, 2, NQ, BANK])
        ld_w, ld_small, stored = c.sems("ld_w", 2), c.sem("ld_small"), c.sems("stored", 2)
        act_own, dve_own = c.sem("act_own"), c.sem("dve_own")
        (consts, hi_ready, lo_ready, product, evacuated, conv_done, silu_done, pool_done) = (
            c.sem(n) for n in ("consts", "hi_ready", "lo_ready", "product", "evacuated", "conv_done",
                               "silu_done", "pool_done"))
        gates_out, gates_in, ends_ready, ends_out, ends_in, prev_ready, prev_out, prev_in = (
            c.sem(n) for n in ("gates_out", "gates_in", "ends_ready", "ends_out", "ends_in", "prev_ready",
                               "prev_out", "prev_in"))
        abs_ready, softplus_ready, neg_m_ready, exps_ready, gates_done, rows_out = (
            c.sem(n) for n in ("abs_ready", "softplus_ready", "neg_m_ready", "exps_ready", "gates_done", "rows_out"))
        block = c.enter_context(nc.Block())
        by_chunk = lambda name: t[name].rearrange("h (c l) -> (h c) l", l=P)
        flat = lambda s: acc[:, s].rearrange("p q n -> p (q n)")

        @block.gpsimd
        def _(g):
            nc.gpsimd.memset(u[:, :, 0:HALO], 0.0).then_inc(consts, 1)
            nc.gpsimd.memset(one[:], 1.0).then_inc(consts, 1)
            nc.gpsimd.memset(prev[:, 0:1], 0.0).then_inc(consts, 1)
            for n in range(HALO):
                nc.gpsimd.memset(inv[:, n:n + 1], 1.0 / (n + 1)).then_inc(consts, 1)

        @block.sync
        def _(sp):
            def load(h, s):
                sp.dma_start(raw[:, s], t["w_in"][2 * h + s]).then_inc(ld_w[s], 16)

            def turn(h, s, ready, count, more=True):
                if more:
                    sp.wait_ge(lo_ready, 2 * h + s + 1)
                    load(h + 1, s)
                sp.wait_ge(ready, count)
                sp.dma_start(t["proj"][2 * h + s], res[:, s]).then_inc(stored[s], 16)

            load(0, 0)
            load(0, 1)
            sp.dma_start(taps[:], t["conv"]).then_inc(ld_small, 16)
            b_gate = t["b_gate"].rearrange("(a d) -> a d", d=1)
            sp.dma_start(bias[0:HEADS], b_gate[0:HEADS]).then_inc(ld_small, 16)
            sp.dma_start(bias[32:32 + HEADS], b_gate[HEADS:2 * HEADS]).then_inc(ld_small, 16)
            sp.wait_ge(lo_ready, 1)
            load(1, 0)
            sp.wait_ge(evacuated, 1)
            sp.dma_start(t["gate_rows"][0:HEADS], res[0:HEADS, 0]).then_inc(gates_out, 16)
            sp.dma_start(t["gate_rows"][HEADS:2 * HEADS], res[32:32 + HEADS, 0]).then_inc(gates_out, 16)
            sp.wait_ge(gates_out, 32)
            sp.dma_start(gi[:], by_chunk("gate_rows")[0:HC]).then_inc(gates_in, 16)
            sp.dma_start(gf[:], by_chunk("gate_rows")[HC:2 * HC]).then_inc(gates_in, 16)
            sp.wait_ge(ends_ready, 2)
            sp.dma_start(t["chunk_ends"], ends[:]).then_inc(ends_out, 16)
            sp.wait_ge(ends_out, 16)
            sp.dma_start(heads[:], t["chunk_ends"].rearrange("(h c) e -> h c e", h=HEADS)).then_inc(ends_in, 16)
            sp.wait_ge(prev_ready, 1)
            sp.dma_start(t["m_prev"], prev[:, 0:NT]).then_inc(prev_out, 16)
            sp.wait_ge(prev_out, 16)
            sp.dma_start(m_prev[:], t["m_prev"].rearrange("h (c a) -> (h c) a", a=1)).then_inc(prev_in, 16)
            sp.wait_ge(neg_m_ready, 1)
            sp.dma_start(by_chunk("neg_m"), gm[:]).then_inc(rows_out, 16)
            sp.wait_ge(exps_ready, 3)
            sp.dma_start(by_chunk("inter"), gf[:]).then_inc(rows_out, 16)
            sp.dma_start(t["decay"].rearrange("(a d) -> a d", d=1), gf[:, P - 1:P]).then_inc(rows_out, 16)
            with sp.Fori(0, 4) as i:
                turn(i, 1, silu_done, 2 * i + 1)
                turn(i + 1, 0, silu_done, 2 * i + 2)
            with sp.Fori(4, 8) as i:
                turn(i, 1, evacuated, 2 * i + 2)
                turn(i + 1, 0, evacuated, 2 * i + 3)
            turn(8, 1, pool_done, 1)
            turn(9, 0, pool_done, 2)
            turn(9, 1, pool_done, 3, more=False)
            turn(10, 0, pool_done, 4, more=False)
            sp.wait_ge(rows_out, 48)
            for s in range(2):
                sp.wait_ge(stored[s], 160)

        def res_free(eng, h, s):
            eng.wait_ge(gates_out, 32)
            at_least(eng, stored[s], 16 * (h if s else h - 1))

        @block.scalar
        def _(act):
            own = Order(act, act_own)
            act.preload_act_table_set(LOG_EXP)

            def high(h, s):
                act.wait_ge(ld_w[s], 16 * (h + 1))
                nc.scalar.activation(w_hi[:, s], raw[:, s], ACT.Copy).then_inc(hi_ready, 1)

            def stage(h, s):
                act.wait_ge(product, 2 * h + s + 1)
                nc.scalar.activation(u[:, s, HALO:], flat(s), ACT.Copy).then_inc(evacuated, 1)

            high(0, 0)
            high(0, 1)
            act.wait_ge(product, 1)
            act.wait_ge(ld_small, 48)
            own.after(nc.scalar.activation(res[0:HEADS, 0], acc[0:HEADS, 0].rearrange("p q n -> p (q n)"),
                                           ACT.Identity, bias=bias[0:HEADS]))
            nc.scalar.activation(res[32:32 + HEADS, 0], acc[32:32 + HEADS, 0].rearrange("p q n -> p (q n)"),
                                 ACT.Identity, bias=bias[32:32 + HEADS]).then_inc(evacuated, 1)
            high(1, 0)
            act.wait_ge(abs_ready, 1)
            own.after(nc.scalar.activation(gb[:], ga[:], ACT.Exp, scale=-1.0))
            nc.scalar.activation(gb[:], gb[:], ACT.Ln, bias=1.0).then_inc(softplus_ready, 1)
            act.wait_ge(gates_done, 2)
            nc.scalar.activation(gb[:], ga[:], ACT.Exp, bias=gm[:, P - 1:P]).then_inc(exps_ready, 1)
            nc.scalar.activation(gi[:], gi[:], ACT.Exp).then_inc(exps_ready, 1)
            nc.scalar.activation(gf[:], gf[:], ACT.Exp).then_inc(exps_ready, 1)
            act.preload_act_table(ACT.Silu)

            def silu_panel(h, s, first=False):
                panel = 2 * h + s
                if not first:
                    act.wait_ge(conv_done, panel - 2)
                stage(h, s)
                high(h + 1, s)
                act.wait_ge(conv_done, panel)
                res_free(act, h, s)
                nc.scalar.activation(res[:, s], (wa if s else wb)[:, 0:SEQ], ACT.Silu).then_inc(silu_done, 1)

            silu_panel(0, 1, True)
            silu_panel(1, 0, True)
            with act.Fori(1, 4) as i:
                silu_panel(i, 1)
                silu_panel(i + 1, 0)

            def plain_panel(h, s, func):
                act.wait_ge(product, 2 * h + s + 1)
                res_free(act, h, s)
                nc.scalar.activation(res[:, s], flat(s), func).then_inc(evacuated, 1)
                high(h + 1, s)

            with act.Fori(4, 6) as i:
                plain_panel(i, 1, ACT.Copy)
                plain_panel(i + 1, 0, ACT.Copy)
            act.preload_act_table(ACT.Sigmoid)
            with act.Fori(6, 8) as i:
                plain_panel(i, 1, ACT.Sigmoid)
                plain_panel(i + 1, 0, ACT.Sigmoid)
            for g in range(4):
                h, s = divmod(17 + g, 2)
                if g >= 2:
                    act.wait_ge(pool_done, g - 1)
                stage(h, s)
                if g < 2:
                    high(h + 1, s)

        @block.vector
        def _(dve):
            own = Order(dve, dve_own)

            def low(h, s):
                dve.wait_ge(hi_ready, 2 * h + s + 1)
                nc.vector.tensor_tensor(w_lo[:, s], raw[:, s], w_hi[:, s].bitcast(F32),
                                        ALU.subtract).then_inc(lo_ready, 1)

            low(0, 0)
            low(0, 1)
            low(1, 0)
            dve.wait_ge(gates_in, 32)
            dve.wait_ge(consts, 3 + HALO)
            nc.vector.scalar_tensor_tensor(ga[:], gf[:], -1.0, gf[:], ALU.mult, ALU.max).then_inc(abs_ready, 1)
            dve.wait_ge(softplus_ready, 1)
            own.after(nc.vector.scalar_tensor_tensor(gf[:], gf[:], 0.0, gb[:], ALU.min, ALU.subtract))
            own.after(nc.vector.tensor_tensor_scan(gb[:], one[:], gf[:], 0.0, ALU.mult, ALU.add))
            own.after(nc.vector.tensor_tensor(ga[:], gi[:], gb[:], ALU.subtract))
            own.after(nc.vector.tensor_tensor_scan(gm[:], ga[:], ga[:], -3e38, ALU.max, ALU.max))
            nc.vector.tensor_copy(ends[:, 0:1], gm[:, P - 1:P]).then_inc(ends_ready, 1)
            nc.vector.tensor_copy(ends[:, 1:2], gb[:, P - 1:P]).then_inc(ends_ready, 1)
            dve.wait_ge(ends_in, 16)
            nc.vector.tensor_tensor_scan(prev[:, 1:], heads[:, :, 0], heads[:, :, 1], 0.0, ALU.max,
                                         ALU.add).then_inc(prev_ready, 1)
            dve.wait_ge(prev_in, 16)
            nc.vector.tensor_scalar(gm[:], gm[:], m_prev[:, 0:1], -1.0, ALU.max, ALU.mult).then_inc(neg_m_ready, 1)
            dve.wait_ge(neg_m_ready, 1)
            nc.vector.tensor_scalar(gf[:], gm[:], m_prev[:, 0:1], None, ALU.add).then_inc(gates_done, 1)
            nc.vector.tensor_tensor(gi[:], gm[:], gb[:], ALU.subtract).then_inc(gates_done, 1)

            dve.wait_ge(ld_small, 48)

            def conv_panel(h, s, first=False):
                panel = 2 * h + s
                low(h + 1, s)
                dve.wait_ge(evacuated, panel + 1)
                if not first:
                    dve.wait_ge(silu_done, panel - 2)
                to = (wa if s else wb)[:, 0:SEQ]
                tap = lambda n: (u[:, s, HALO - 3 + n:HALO - 3 + n + SEQ], taps[:, bass.ds(panel - 1, 1), n])
                own.after(nc.vector.tensor_scalar(to, tap(0)[0], tap(0)[1], None, ALU.mult))
                for n in range(1, 4):
                    ins = nc.vector.scalar_tensor_tensor(to, tap(n)[0], tap(n)[1], to, ALU.mult, ALU.add)
                    if n < 3:
                        own.after(ins)
                ins.then_inc(conv_done, 1)

            conv_panel(0, 1, True)
            conv_panel(1, 0, True)
            with dve.Fori(1, 4) as i:
                own.start(i - 1, 6)
                conv_panel(i, 1)
                conv_panel(i + 1, 0)
            own.end(3)
            with dve.Fori(4, 8) as i:
                low(i + 1, 1)
                low(i + 2, 0)
            dve.wait_ge(silu_done, 8)
            for g, window in enumerate(POOL_WINDOWS):
                h, s = divmod(17 + g, 2)
                if g < 2:
                    low(h + 1, s)
                dve.wait_ge(evacuated, 2 * h + s + 1)
                at, total, other, step = 1, u[:, s], wa, 1
                while step < window:
                    own.after(nc.vector.tensor_tensor(other[:, at:], total[:, at:],
                                                      total[:, at - step:HALO + SEQ - step], ALU.add))
                    total, other = other, (wb if other is wa else wa)
                    step *= 2
                    at += step
                res_free(dve, h, s)
                own.after(nc.vector.scalar_tensor_tensor(res[:, s], total[:, HALO:], 1.0 / window, u[:, s, HALO:],
                                                         ALU.mult, ALU.subtract))
                own.after(nc.vector.tensor_tensor(edge[:], total[:, HALO:2 * HALO], inv[:], ALU.mult))
                nc.vector.tensor_tensor(res[:, s, 0:window - 1], edge[:, 0:window - 1],
                                        u[:, s, HALO:HALO + window - 1], ALU.subtract).then_inc(pool_done, 1)

        @block.tensor
        def _(pe):
            def panel(h, s, first=False):
                pe.wait_ge(lo_ready, 2 * h + s + 1)
                if not first:
                    at_least(pe, evacuated, 2 * h + s - 1)
                for q in range(NQ):
                    at = slice(q * BANK, (q + 1) * BANK)
                    for k in range(KT):
                        nc.tensor.matmul(acc[:, s, q], w_hi[:, s, k], h_hi[:, k, at], start=(k == 0), stop=False)
                        nc.tensor.matmul(acc[:, s, q], w_hi[:, s, k], h_lo[:, k, at], start=False, stop=False)
                        last = nc.tensor.matmul(acc[:, s, q], w_lo[:, s, k], h_hi[:, k, at], start=False,
                                                stop=(k == KT - 1))
                last.then_inc(product, 1)

            panel(0, 0, True)
            panel(0, 1, True)
            panel(1, 0)
            with pe.Fori(1, 10) as i:
                panel(i, 1)
                panel(i + 1, 0)


def mlstm_out(nc, t, ident, gate_rows):
    with Scope(nc, "mo") as c:
        DA = DH + 1
        raw = c.sb("raw", [P, 2, D])
        w_hi, w_lo = c.sb("w_hi", [P, KT, D], FR), c.sb("w_lo", [P, KT, D], FR)
        w_gain = c.sb("w_gain", [P, KT])
        gain = c.sb("gain", [P, D])
        qkv, od = c.sb("qkv", [P, 2, 3, HEADS, P]), c.sb("od", [P, 2, 2, HEADS, P])
        neg_m, inter = c.sb("neg_m", [P, 2, HEADS, P]), c.sb("inter", [P, 2, HEADS, P])
        cols, decay = c.sb("cols", [P, 3, HEADS, NT]), c.sb("decay", [P, HEADS, NT])
        cap = c.sb("cap", [P, P])
        probs, scores, qs = (c.sb(n, [P, HEADS, P]) for n in ("probs", "scores", "qs"))
        vn, kn = c.sb("vn", [P, HEADS, DA]), c.sb("kn", [P, HEADS, DH])
        state = c.sb("state", [P, HEADS, DA])
        heads = c.sb("heads", [P, HEADS, DH])
        gated = c.sb("gated", [P, HEADS, P])
        mix_hi, mix_lo = c.sb("mix_hi", [P, 2, KT, P], FR), c.sb("mix_lo", [P, 2, KT, P], FR)
        x, x1 = c.sb("x", [P, 2, D]), c.sb("x1", [P, 2, D])
        normed, junk = c.sb("normed", [P, D]), c.sb("junk", [P, D])
        h_ss, h_y0, h_tmp, h_rs, den, h_var = (c.sb(n, [P, HEADS]) for n in ("h_ss", "h_y0", "h_tmp", "h_rs", "den", "h_var"))
        y_ss, y_y0, y_tmp, y_rs = (c.sb(n, [P, 1]) for n in ("y_ss", "y_y0", "y_tmp", "y_rs"))
        turn_ps = c.ps("turn", [P, HEADS, P])
        kv_ps = c.ps("kv", [P, 2, BANK])
        s_ps = c.ps("s", [P, HEADS, P])
        n_ps = c.ps("n", [P, 2, BANK])
        y_ps = c.ps("y", [P, 2, BANK])
        k_turn_ps = kv_ps[:, 0].rearrange("p (h e) -> p h e", h=HEADS)
        pairs = lambda ps: ps[:, :, 0:2 * DA].rearrange("p b (h e) -> p b h e", h=2)
        one_head = lambda ps, h, n: ps[:, h // 2, (h % 2) * DA:(h % 2) * DA + n]
        by_pair = lambda ap: ap.rearrange("p (b h) e -> p b h e", b=2)
        two = lambda ap: ap.rearrange("p (b h) -> p b h", b=2)

        ld_w, ld_const = c.sems("ld_w", 2), c.sem("ld_const")
        ld_qkv, ld_bc, ld_od, ld_x = (c.sems(n, 2) for n in ("ld_qkv", "ld_bc", "ld_od", "ld_x"))
        stored = c.sems("stored", 2)
        act_own, dve_own = c.sem("act_own"), c.sem("dve_own")
        consts, w_hi_ready, w_lo_ready, cols_turned, cols_ready = (
            c.sem(n) for n in ("consts", "w_hi_ready", "w_lo_ready", "cols_turned", "cols_ready"))
        v_turned, k_turned, s_done, n_done, kv_done, m_turned, y_done = (
            c.sem(n) for n in ("v_turned", "k_turned", "s_done", "n_done", "kv_done", "m_turned", "y_done"))
        vn_ready, probs_ready, squares, h_guess, d_hi, m_hi, y_guess = (
            c.sem(n) for n in ("vn_ready", "probs_ready", "squares", "h_guess", "d_hi", "m_hi", "y_guess"))
        args_ready, kn_ready, qs_ready, scores_ready, var_ready, heads_ready, gated_ready = (
            c.sem(n) for n in ("args_ready", "kn_ready", "qs_ready", "scores_ready", "var_ready", "heads_ready",
                               "gated_ready"))
        mix_ready, y_read, x1_ready, state_ready = (c.sem(n) for n in ("mix_ready", "y_read", "x1_ready", "state_ready"))
        block = c.enter_context(nc.Block())

        x_d = t["x"].rearrange("(t p) d -> t p d", p=P)
        x1_d = t["x1"].rearrange("(t p) d -> t p d", p=P)
        chunk = lambda lo, hi, cc: t["proj"][lo:hi, :, bass.ds(cc * P, P)].rearrange("h p l -> p h l")

        def turns(eng, body, own=None, steps=0):
            body(0, 0, True, False, False)
            body(0, 1, True, True, False)
            body(1, 0, True, True, True)
            body(1, 1, True, True, True)
            with eng.Fori(2, NT // 2) as i:
                if own:
                    own.start(i - 2, steps)
                body(i, 0, True, True, True)
                body(i, 1, True, True, True)
            if own:
                own.end(NT // 2 - 2)
            body(NT // 2, 0, False, True, True)
            body(NT // 2, 1, False, False, True)

        @block.gpsimd
        def _(g):
            nc.gpsimd.memset(w_gain[:, 0:4], 1.0).then_inc(consts, 1)
            nc.gpsimd.memset(vn[:, :, DH:], 1.0).then_inc(consts, 1)
            nc.gpsimd.memset(state[:], 0.0).then_inc(consts, 1)
            nc.gpsimd.memset(cap[:], 0.0).then_inc(consts, 1)
            g.wait_ge(consts, 4)
            nc.gpsimd.affine_select(out=cap[:], in_=cap[:], compare_op=ALU.is_ge, fill=LOW, base=0,
                                    pattern=[[1, P]], channel_multiplier=-1).then_inc(consts, 1)

        @block.sync
        def _(sp):
            def load_w(k):
                src = t["pool_out"][k * P:(k + 1) * P] if k < 4 else t["w_out"][k * P:(k + 1) * P]
                sp.dma_start(raw[:, k % 2], src).then_inc(ld_w[k % 2], 16)

            def load_chunk(cc, s):
                for j in range(3):
                    sp.dma_start(qkv[:, s, j], chunk(1 + 4 * j, 5 + 4 * j, cc)).then_inc(ld_qkv[s], 16)
                for to, name in ((neg_m, "neg_m"), (inter, "inter")):
                    sp.dma_start(to[:, s], t[name][:, bass.ds(cc * P, P)].partition_broadcast(P)).then_inc(ld_bc[s], 16)

            def load_od(cc, s):
                for j in range(2):
                    sp.dma_start(od[:, s, j], chunk(13 + 4 * j, 17 + 4 * j, cc)).then_inc(ld_od[s], 16)

            load_chunk(0, 0)
            sp.dma_start(decay[:].rearrange("p h c -> p (h c)"), t["decay"].partition_broadcast(P)).then_inc(ld_const, 16)
            sp.dma_start(w_gain[:, 4:], t["mlstm_norm_g_cols"]).then_inc(ld_const, 16)
            load_w(0)
            load_w(1)
            load_chunk(1, 1)
            sp.dma_start(gain[:], rows_all(t["g_mix_post"])).then_inc(ld_const, 16)
            for k in range(2, KT):
                sp.wait_ge(w_lo_ready, k - 1)
                load_w(k)

            def body(h, s, now, before, out):
                cc = 2 * h + s
                if now:
                    if out:
                        sp.wait_ge(mix_ready, cc - 1)
                    load_od(cc, s)
                    sp.dma_start(x[:, s], x_d[cc]).then_inc(ld_x[s], 16) if not out else None
                if out:
                    sp.wait_ge(x1_ready, cc - 1)
                    sp.dma_start(x1_d[cc - 2], x1[:, s]).then_inc(stored[s], 16)
                    if now:
                        sp.dma_start(x[:, s], x_d[cc]).then_inc(ld_x[s], 16)

            def ahead(h, s):
                cc = 2 * h + s
                sp.wait_ge(k_turned, cc + 1)
                sp.wait_ge(qs_ready, cc + 1)
                load_chunk(cc + 2, s)

            def both(h, s, now, before, out):
                body(h, s, now, before, out)
                if now and ahead_ok[0]:
                    ahead(h, s)

            ahead_ok = [True]
            both(0, 0, True, False, False)
            both(0, 1, True, True, False)
            both(1, 0, True, True, True)
            both(1, 1, True, True, True)
            with sp.Fori(2, NT // 2 - 1) as i:
                both(i, 0, True, True, True)
                both(i, 1, True, True, True)
            ahead_ok[0] = False
            both(NT // 2 - 1, 0, True, True, True)
            both(NT // 2 - 1, 1, True, True, True)
            both(NT // 2, 0, False, True, True)
            both(NT // 2, 1, False, False, True)
            for s in range(2):
                sp.wait_ge(stored[s], 16 * (NT // 2))

        @block.scalar
        def _(act):
            own = Order(act, act_own)
            act.preload_act_table_set(LOG_EXP)
            act.wait_ge(cols_turned, 1)
            nc.scalar.activation(cols[:].rearrange("p k h c -> p (k h c)"),
                                 turn_ps[:].rearrange("p h e -> p (h e)")[:, 0:3 * HC], ACT.Copy).then_inc(cols_ready, 1)
            act.wait_ge(ld_const, 48)
            act.wait_ge(consts, 1)

            def body(h, s, now, before, out):
                cc = 2 * h + s
                if now:
                    act.wait_ge(v_turned, cc + 1)
                    if before:
                        act.wait_ge(kv_done, cc)
                    nc.scalar.activation(vn[:, :, 0:DH], turn_ps[:], ACT.Copy).then_inc(vn_ready, 1)
                    act.wait_ge(args_ready, cc + 1)
                    nc.scalar.activation(probs[:], probs[:], ACT.Exp).then_inc(probs_ready, 1)
                if not out:
                    for k in range(4 * s, 4 * s + 4):
                        act.wait_ge(ld_w[k % 2], 16 * (k // 2 + 1))
                        nc.scalar.activation(w_hi[:, k], raw[:, k % 2], ACT.Copy,
                                             scale=w_gain[:, k:k + 1]).then_inc(w_hi_ready, 1)
                if before:
                    act.wait_ge(n_done, cc)
                    for hd in range(HEADS):
                        ins = nc.scalar.activation(junk[:, hd * DH:(hd + 1) * DH], one_head(n_ps, hd, DH), ACT.Square,
                                                   accum_out=h_ss[:, hd:hd + 1])
                    ins.then_inc(squares, 1)
                    act.wait_ge(var_ready, cc)
                    rsqrt_start(nc, own, h_y0[:], h_var[:], 1.0 / DH, EPS).then_inc(h_guess, 1)
                    act.wait_ge(ld_od[1 - s], 32 * (h + s))
                    if out:
                        at_least(act, y_done, cc - 2)
                    nc.scalar.activation(mix_hi[:, 1 - s, 0:4], od[:, 1 - s, 1], ACT.Copy).then_inc(d_hi, 1)
                if out:
                    act.wait_ge(y_done, cc - 1)
                    own.after(nc.scalar.activation(junk[:], y_ps[:].rearrange("p a n -> p (a n)"), ACT.Square,
                                                   accum_out=y_ss[:]))
                    rsqrt_start(nc, own, y_y0[:], y_ss[:], 1.0 / D, EPS).then_inc(y_guess, 1)
                if before:
                    act.wait_ge(gated_ready, cc)
                    nc.scalar.activation(mix_hi[:, 1 - s, 4:], gated[:], ACT.Copy).then_inc(m_hi, 1)

            turns(act, body, own, 6)

        @block.vector
        def _(dve):
            own = Order(dve, dve_own)
            dve.wait_ge(ld_const, 48)
            dve.wait_ge(consts, 5)
            dve.wait_ge(cols_ready, 1)

            def body(h, s, now, before, out):
                cc = 2 * h + s
                at = bass.ds(cc, 1)
                if now:
                    dve.wait_ge(ld_bc[s], 32 * (h + 1))
                    for hd in range(HEADS):
                        ins = nc.vector.scalar_tensor_tensor(probs[:, hd], neg_m[:, s, hd], cols[:, 0, hd, at], cap[:],
                                                             ALU.add, ALU.min)
                    ins.then_inc(args_ready, 1)
                    dve.wait_ge(k_turned, cc + 1)
                    if before:
                        dve.wait_ge(kv_done, cc)
                    nc.vector.tensor_tensor(kn[:], k_turn_ps, cols[:, 1, :, at].to_broadcast([P, HEADS, DH]),
                                            ALU.mult).then_inc(kn_ready, 1)
                    nc.vector.scalar_tensor_tensor(qs[:], inter[:, s], DH ** -0.5, qkv[:, s, 0], ALU.mult,
                                                   ALU.mult).then_inc(qs_ready, 1)
                    dve.wait_ge(s_done, cc + 1)
                    dve.wait_ge(probs_ready, cc + 1)
                    nc.vector.scalar_tensor_tensor(scores[:], s_ps[:], DH ** -0.5, probs[:], ALU.mult,
                                                   ALU.mult).then_inc(scores_ready, 1)
                if not out:
                    for k in range(4 * s, 4 * s + 4):
                        dve.wait_ge(w_hi_ready, k + 1)
                        nc.vector.scalar_tensor_tensor(w_lo[:, k], raw[:, k % 2], w_gain[:, k:k + 1],
                                                       w_hi[:, k].bitcast(F32), ALU.mult,
                                                       ALU.subtract).then_inc(w_lo_ready, 1)
                if before:
                    last = bass.ds(cc - 1, 1)
                    dve.wait_ge(squares, cc)
                    own.after(nc.vector.tensor_tensor(two(den[:]), pairs(n_ps)[:, :, :, DH],
                                                      two(cols[:, 2, :, last].rearrange("p h a -> p (h a)")), ALU.max))
                    own.after(nc.vector.scalar_tensor_tensor(two(den[:]), pairs(n_ps)[:, :, :, DH], -1.0, two(den[:]),
                                                             ALU.mult, ALU.max))
                    own.after(nc.vector.reciprocal(den[:], den[:]))
                    own.after(nc.vector.tensor_tensor(h_var[:], h_ss[:], den[:], ALU.mult))
                    nc.vector.tensor_tensor(h_var[:], h_var[:], den[:], ALU.mult).then_inc(var_ready, 1)
                    dve.wait_ge(h_guess, cc)
                    own.after(rsqrt_end(nc, own, h_rs[:], h_y0[:], h_var[:], h_tmp[:], 1.0 / DH, EPS))
                    own.after(nc.vector.tensor_tensor(h_rs[:], h_rs[:], den[:], ALU.mult))
                    if out:
                        dve.wait_ge(m_turned, cc - 1)
                    nc.vector.tensor_tensor(by_pair(heads[:]), pairs(n_ps)[:, :, :, 0:DH],
                                            two(h_rs[:]).unsqueeze(3).to_broadcast([P, 2, 2, DH]),
                                            ALU.mult).then_inc(heads_ready, 1)
                    dve.wait_ge(d_hi, cc)
                    nc.vector.tensor_tensor(mix_lo[:, 1 - s, 0:4], od[:, 1 - s, 1], mix_hi[:, 1 - s, 0:4].bitcast(F32),
                                            ALU.subtract)
                    dve.wait_ge(m_turned, cc)
                    nc.vector.tensor_tensor(gated[:], turn_ps[:], od[:, 1 - s, 0], ALU.mult).then_inc(gated_ready, 1)
                if out:
                    dve.wait_ge(y_guess, cc - 1)
                    own.after(rsqrt_end(nc, own, y_rs[:], y_y0[:], y_ss[:], y_tmp[:], 1.0 / D, EPS))
                    nc.vector.scalar_tensor_tensor(normed[:], y_ps[:].rearrange("p a n -> p (a n)"), y_rs[:],
                                                   gain[:], ALU.mult, ALU.mult).then_inc(y_read, 1)
                if before:
                    dve.wait_ge(m_hi, cc)
                    nc.vector.tensor_tensor(mix_lo[:, 1 - s, 4:], gated[:], mix_hi[:, 1 - s, 4:].bitcast(F32),
                                            ALU.subtract).then_inc(mix_ready, 1)
                if now:
                    dve.wait_ge(kv_done, cc + 1)
                    for hd in range(HEADS):
                        ins = nc.vector.scalar_tensor_tensor(state[:, hd], state[:, hd], decay[:, hd, at],
                                                             one_head(kv_ps, hd, DA), ALU.mult, ALU.add)
                    ins.then_inc(state_ready, 1)
                if out:
                    dve.wait_ge(y_read, cc - 1)
                    dve.wait_ge(ld_x[s], 16 * h)
                    at_least(dve, stored[s], 16 * (h - 1))
                    nc.vector.tensor_tensor(x1[:, s], normed[:], x[:, s], ALU.add).then_inc(x1_ready, 1)

            turns(dve, body, own, 30)

        @block.tensor
        def _(pe):
            for j, rows in enumerate((gate_rows[0], gate_rows[1], gate_rows[2])):
                ins = nc.tensor.transpose(turn_ps[:].rearrange("p h e -> p (h e)")[:, j * HC:(j + 1) * HC], rows[:],
                                          ident[0:HC, 0:HC])
            ins.then_inc(cols_turned, 1)
            pe.wait_ge(cols_ready, 1)

            def body(h, s, now, before, out):
                cc = 2 * h + s
                if now:
                    pe.wait_ge(ld_qkv[s], 48 * (h + 1))
                    if out:
                        pe.wait_ge(gated_ready, cc - 1)
                    for hd in range(HEADS):
                        ins = nc.tensor.transpose(turn_ps[:, hd], qkv[:, s, 2, hd], ident[:])
                    ins.then_inc(v_turned, 1)
                    if before:
                        pe.wait_ge(scores_ready, cc)
                    for hd in range(HEADS):
                        ins = nc.tensor.matmul(s_ps[:, hd], qkv[:, s, 1, hd], qkv[:, s, 0, hd], start=True, stop=True)
                    ins.then_inc(s_done, 1)
                if out:
                    pe.wait_ge(mix_ready, cc - 1)
                    at_least(pe, y_read, cc - 2)
                    pe.wait_ge(w_lo_ready, KT)
                for half in range(2):
                    if half and now:
                        if before:
                            pe.wait_ge(state_ready, cc)
                        for hd in range(HEADS):
                            ins = nc.tensor.transpose(k_turn_ps[:, hd], qkv[:, s, 1, hd], ident[:])
                        ins.then_inc(k_turned, 1)
                    if out:
                        n = slice(half * BANK, (half + 1) * BANK)
                        for k in range(KT):
                            nc.tensor.matmul(y_ps[:, half], mix_hi[:, s, k], w_hi[:, k, n], start=(k == 0), stop=False)
                            nc.tensor.matmul(y_ps[:, half], mix_hi[:, s, k], w_lo[:, k, n], start=False, stop=False)
                            ins = nc.tensor.matmul(y_ps[:, half], mix_lo[:, s, k], w_hi[:, k, n], start=False,
                                                   stop=(k == KT - 1))
                        if half:
                            ins.then_inc(y_done, 1)
                if before:
                    pe.wait_ge(heads_ready, cc)
                    if now:
                        pe.wait_ge(vn_ready, cc + 1)
                    for hd in range(HEADS):
                        ins = nc.tensor.transpose(turn_ps[:, hd], heads[:, hd], ident[:])
                    ins.then_inc(m_turned, 1)
                if now:
                    pe.wait_ge(vn_ready, cc + 1)
                    pe.wait_ge(scores_ready, cc + 1)
                    pe.wait_ge(kn_ready, cc + 1)
                    for hd in range(HEADS):
                        nc.tensor.matmul(one_head(n_ps, hd, DA), scores[:, hd], vn[:, hd], start=True, stop=False)
                        ins = nc.tensor.matmul(one_head(n_ps, hd, DA), qs[:, hd], state[:, hd], start=False, stop=True)
                    ins.then_inc(n_done, 1)
                    for hd in range(HEADS):
                        ins = nc.tensor.matmul(one_head(kv_ps, hd, DA), kn[:, hd], vn[:, hd], start=True, stop=True)
                    ins.then_inc(kv_done, 1)

            turns(pe, body)

def cross(nc, t, ident):
    with Scope(nc, "cr") as c:
        a_hi, a_lo = c.sb("a_hi", [P, KT, D], FR), c.sb("a_lo", [P, KT, D], FR)
        b_hi, b_lo = c.sb("b_hi", [P, KT, D], FR), c.sb("b_lo", [P, KT, D], FR)
        x2 = c.sb("x2", [P, 2, D])
        raw = x2
        xa, xb = c.sb("xa", [P, 2, D]), c.sb("xb", [P, D])
        h_buffer, probs, h3 = c.sb("h", [P, D]), c.sb("probs", [P, D]), c.sb("h3", [P, D])
        junk, gain = c.sb("junk", [P, D]), c.sb("gain", [P, D])
        g_ffn = c.sb("g_ffn", [P, KT])
        h_hi, h_lo = c.sb("h_hi", [P, 2, KT, P], FR), c.sb("h_lo", [P, 2, KT, P], FR)
        p_hi, p_lo = c.sb("p_hi", [P, 2, KT, P], FR), c.sb("p_lo", [P, 2, KT, P], FR)
        h3_t = c.sb("h3_t", [P, KT, P])
        x_st, y_st, z_st = ([c.sb(a + n, [P, 1]) for n in ("ss", "y0", "tmp", "rs")] for a in ("x_", "y_", "z_"))
        neg_max, sums = c.sb("neg_max", [P, HEADS]), c.sb("sums", [P, HEADS])
        s_ps, y_ps = c.ps("s", [P, 2, BANK]), c.ps("y", [P, 2, BANK])
        tr, tr3 = c.ps("tr", [P, KT, P]), c.ps("tr3", [P, KT, P])
        flat = lambda ps: ps[:].rearrange("p a n -> p (a n)")
        by_head = lambda ap: ap.rearrange("p (h m) -> p h m", h=HEADS)

        ld_w, ld_const, ld_xa, ld_xb = c.sems("ld_w", 2), c.sem("ld_const"), c.sems("ld_xa", 2), c.sem("ld_xb")
        stored, stored3 = c.sems("stored", 2), c.sem("stored3")
        act_own, dve_own = c.sem("act_own"), c.sem("dve_own")
        w_hi_ready, w_lo_ready = c.sem("w_hi_ready"), c.sem("w_lo_ready")
        x_guess, y_guess, z_guess, h_hi_ready, p_hi_ready, exps = (
            c.sem(n) for n in ("x_guess", "y_guess", "z_guess", "h_hi_ready", "p_hi_ready", "exps"))
        h_ready, h_lo_ready, max_ready, probs_ready, p_lo_ready, x2_ready, h3_ready, h3_t_ready = (
            c.sem(n) for n in ("h_ready", "h_lo_ready", "max_ready", "probs_ready", "p_lo_ready", "x2_ready",
                               "h3_ready", "h3_t_ready"))
        h_turned, p_turned, x_turned, s_done, y_done = (
            c.sem(n) for n in ("h_turned", "p_turned", "x_turned", "s_done", "y_done"))
        block = c.enter_context(nc.Block())
        tiles = lambda name: t[name].rearrange("(t p) d -> t p d", p=P)

        class Parts:

            def __init__(self, j=None):
                inner = j is None
                self.scores = inner or j < NT
                self.ahead = inner or j + 1 < NT
                self.ahead2 = inner or j + 2 < NT
                self.probs = inner or 1 <= j <= NT
                self.out = inner or 2 <= j <= NT + 1
                self.post = inner or 3 <= j
                self.j = j

        def turns(eng, body, own=None, steps=0):
            for j in range(6):
                body(j // 2, j % 2, Parts(j))
            with eng.Fori(3, NT // 2 - 1) as i:
                if own:
                    own.start(i - 3, steps)
                body(i, 0, Parts())
                body(i, 1, Parts())
            if own:
                own.end(NT // 2 - 4)
            for j in range(NT - 2, NT + 3):
                body(j // 2, j % 2, Parts(j))

        @block.sync
        def _(sp):
            def load_w(k):
                src = t["a_mat"] if k < KT else t["b_mat"]
                sp.dma_start(raw[:, k % 2], src[(k % KT) * P:(k % KT + 1) * P]).then_inc(ld_w[k % 2], 16)

            def load_xa(j, s):
                sp.dma_start(xa[:, s], tiles("x1")[j]).then_inc(ld_xa[s], 16)

            load_w(0)
            load_w(1)
            load_xa(0, 0)
            load_xa(1, 1)
            sp.dma_start(gain[:], rows_all(t["g_xattn_post"])).then_inc(ld_const, 16)
            sp.dma_start(g_ffn[:], t["g_ffn_pre_cols"]).then_inc(ld_const, 16)

            def load_ws(ks):
                for k in ks:
                    sp.wait_ge(w_lo_ready, k - 1)
                    load_w(k)

            load_ws(range(2, KT + 2))

            def body(h, s, p):
                j = 2 * h + s
                if p.post:
                    sp.wait_ge(x2_ready, j - 2)
                    sp.dma_start(tiles("x2")[j - 3], x2[:, 1 - s]).then_inc(stored[1 - s], 16)
                if p.out:
                    sp.dma_start(xb[:], tiles("x1")[j - 2]).then_inc(ld_xb, 16)
                if p.ahead2:
                    sp.wait_ge(h_ready, j + 1)
                    load_xa(j + 2, s)
                if p.j in (0, 1):
                    load_ws(range(KT + 2 + 4 * p.j, min(KT + 6 + 4 * p.j, 2 * KT)))
                if p.post:
                    sp.wait_ge(h3_t_ready, j - 2)
                    sp.dma_start(t["h3_t"][:, :, bass.ds((j - 3) * P, P)].rearrange("k p l -> p k l"),
                                 h3_t[:]).then_inc(stored3, 16)

            turns(sp, body)
            for s in range(2):
                sp.wait_ge(stored[s], 16 * (NT // 2))
            sp.wait_ge(stored3, 16 * NT)

        @block.scalar
        def _(act):
            own = Order(act, act_own)
            act.preload_act_table_set(LOG_EXP)

            def split(k):
                act.wait_ge(ld_w[k % 2], 16 * (k // 2 + 1))
                nc.scalar.activation((a_hi if k < KT else b_hi)[:, k % KT], raw[:, k % 2],
                                     ACT.Copy).then_inc(w_hi_ready, 1)

            def stats(h, s):
                j = 2 * h + s
                act.wait_ge(ld_xa[s], 16 * (h + 1))
                if not (isinstance(j, int) and j == 0):
                    act.wait_ge(h_ready, j)
                own.after(nc.scalar.activation(junk[:], xa[:, s], ACT.Square, accum_out=x_st[0][:]))
                rsqrt_start(nc, own, x_st[1][:], x_st[0][:], 1.0 / D, EPS).then_inc(x_guess, 1)

            def high_h(j, s):
                act.wait_ge(h_turned, j + 1)
                nc.scalar.activation(h_hi[:, s], tr[:], ACT.Copy).then_inc(h_hi_ready, 1)

            for k in range(KT):
                split(k)
            stats(0, 0)
            high_h(0, 0)
            stats(0, 1)

            def body(h, s, p):
                j = 2 * h + s
                if p.j in (0, 1):
                    for k in range(KT + 4 * p.j, KT + 4 * p.j + 4):
                        split(k)
                if p.post:
                    act.wait_ge(y_done, j - 2)
                    own.after(nc.scalar.activation(junk[:], flat(y_ps), ACT.Square, accum_out=y_st[0][:]))
                    rsqrt_start(nc, own, y_st[1][:], y_st[0][:], 1.0 / D, EPS).then_inc(y_guess, 1)
                    act.wait_ge(x2_ready, j - 2)
                    own.after(nc.scalar.activation(junk[:], x2[:, 1 - s], ACT.Square, accum_out=z_st[0][:]))
                    rsqrt_start(nc, own, z_st[1][:], z_st[0][:], 1.0 / D, EPS).then_inc(z_guess, 1)
                if p.ahead:
                    high_h(j + 1, 1 - s)
                if p.ahead2:
                    stats(h + 1, s)
                if p.probs:
                    act.wait_ge(p_turned, j)
                    nc.scalar.activation(p_hi[:, 1 - s], tr[:], ACT.Copy).then_inc(p_hi_ready, 1)
                if p.scores:
                    act.wait_ge(max_ready, j + 1)
                    for hd in range(HEADS):
                        at = slice(hd * N_MEM, (hd + 1) * N_MEM)
                        ins = nc.scalar.activation(probs[:, at], flat(s_ps)[:, at], ACT.Exp,
                                                   bias=neg_max[:, hd:hd + 1], accum_out=sums[:, hd:hd + 1])
                    ins.then_inc(exps, 1)

            turns(act, body, own, 12)

        @block.vector
        def _(dve):
            own = Order(dve, dve_own)

            def split(k):
                dve.wait_ge(w_hi_ready, k + 1)
                hi, lo = (a_hi, a_lo) if k < KT else (b_hi, b_lo)
                nc.vector.tensor_tensor(lo[:, k % KT], raw[:, k % 2], hi[:, k % KT].bitcast(F32),
                                        ALU.subtract).then_inc(w_lo_ready, 1)

            def normalise(j, s):
                dve.wait_ge(x_guess, j + 1)
                own.after(rsqrt_end(nc, own, x_st[3][:], x_st[1][:], x_st[0][:], x_st[2][:], 1.0 / D, EPS))
                if not (isinstance(j, int) and j == 0):
                    dve.wait_ge(h_turned, j)
                nc.vector.tensor_scalar(h_buffer[:], xa[:, s], x_st[3][:], None, ALU.mult).then_inc(h_ready, 1)

            def low_h(j, s):
                dve.wait_ge(h_hi_ready, j + 1)
                nc.vector.tensor_tensor(h_lo[:, s], tr[:], h_hi[:, s].bitcast(F32), ALU.subtract).then_inc(h_lo_ready, 1)

            for k in range(KT):
                split(k)
            normalise(0, 0)
            low_h(0, 0)
            dve.wait_ge(ld_const, 32)

            def body(h, s, p):
                j = 2 * h + s
                if p.j in (0, 1):
                    for k in range(KT + 4 * p.j, KT + 4 * p.j + 4):
                        split(k)
                if p.ahead:
                    normalise(j + 1, 1 - s)
                if p.post:
                    dve.wait_ge(y_guess, j - 2)
                    own.after(rsqrt_end(nc, own, y_st[3][:], y_st[1][:], y_st[0][:], y_st[2][:], 1.0 / D, EPS))
                    at_least(dve, stored[1 - s], 16 * (h - 1 if s else h - 2))
                    own.after(nc.vector.scalar_tensor_tensor(x2[:, 1 - s], flat(y_ps), y_st[3][:], gain[:], ALU.mult,
                                                             ALU.mult))
                    dve.wait_ge(ld_xb, 16 * (j - 2))
                    nc.vector.tensor_tensor(x2[:, 1 - s], x2[:, 1 - s], xb[:], ALU.add).then_inc(x2_ready, 1)
                    dve.wait_ge(z_guess, j - 2)
                    own.after(rsqrt_end(nc, own, z_st[3][:], z_st[1][:], z_st[0][:], z_st[2][:], 1.0 / D, EPS))
                    if p.j != 3:
                        dve.wait_ge(x_turned, j - 3)
                    nc.vector.tensor_scalar(h3[:], x2[:, 1 - s], z_st[3][:], None, ALU.mult).then_inc(h3_ready, 1)
                if p.ahead:
                    low_h(j + 1, 1 - s)
                if p.scores:
                    dve.wait_ge(s_done, j + 1)
                    if p.j != 0:
                        dve.wait_ge(exps, j)
                    own.after(nc.vector.tensor_reduce(neg_max[:], by_head(flat(s_ps)), AX_X, ALU.max))
                    nc.vector.tensor_scalar(neg_max[:], neg_max[:], -1.0, None, ALU.mult).then_inc(max_ready, 1)
                if p.post:
                    dve.wait_ge(x_turned, j - 2)
                    if p.j != 3:
                        dve.wait_ge(stored3, 16 * (j - 3))
                    nc.vector.tensor_tensor(h3_t[:], tr3[:], g_ffn[:].unsqueeze(2).to_broadcast([P, KT, P]),
                                            ALU.mult).then_inc(h3_t_ready, 1)
                if p.probs:
                    dve.wait_ge(p_hi_ready, j)
                    nc.vector.tensor_tensor(p_lo[:, 1 - s], tr[:], p_hi[:, 1 - s].bitcast(F32),
                                            ALU.subtract).then_inc(p_lo_ready, 1)
                if p.scores:
                    dve.wait_ge(exps, j + 1)
                    own.after(nc.vector.reciprocal(sums[:], sums[:]))
                    nc.vector.tensor_tensor(by_head(probs[:]), by_head(probs[:]),
                                            sums[:].unsqueeze(2).to_broadcast([P, HEADS, N_MEM]),
                                            ALU.mult).then_inc(probs_ready, 1)

            turns(dve, body, own, 36)

        @block.tensor
        def _(pe):
            def turn_h(j, s):
                pe.wait_ge(h_ready, j + 1)
                if not (isinstance(j, int) and j < 3):
                    pe.wait_ge(p_lo_ready, j - 2)
                for k in range(KT):
                    ins = nc.tensor.transpose(tr[:, k], h_buffer[:, k * P:(k + 1) * P], ident[:])
                ins.then_inc(h_turned, 1)

            def product(out, hi, lo, w_hi, w_lo, n):
                for k in range(KT):
                    nc.tensor.matmul(out, hi[:, k], w_hi[:, k, n], start=(k == 0), stop=False)
                    nc.tensor.matmul(out, hi[:, k], w_lo[:, k, n], start=False, stop=False)
                    ins = nc.tensor.matmul(out, lo[:, k], w_hi[:, k, n], start=False, stop=(k == KT - 1))
                return ins

            turn_h(0, 0)

            def body(h, s, p):
                j = 2 * h + s
                for half in range(2):
                    if p.scores:
                        if half == 0:
                            pe.wait_ge(h_lo_ready, j + 1)
                            pe.wait_ge(w_lo_ready, KT)
                            if p.j != 0:
                                pe.wait_ge(exps, j)
                        ins = product(s_ps[:, half], h_hi[:, s], h_lo[:, s], a_hi, a_lo,
                                      slice(half * BANK, (half + 1) * BANK))
                        if half:
                            ins.then_inc(s_done, 1)
                    if half == 0 and p.ahead:
                        turn_h(j + 1, 1 - s)
                if p.post:
                    pe.wait_ge(h3_ready, j - 2)
                    if p.j != 3:
                        pe.wait_ge(h3_t_ready, j - 3)
                    for k in range(KT):
                        ins = nc.tensor.transpose(tr3[:, k], h3[:, k * P:(k + 1) * P], ident[:])
                    ins.then_inc(x_turned, 1)
                if p.probs:
                    pe.wait_ge(probs_ready, j)
                    if p.ahead:
                        pe.wait_ge(h_lo_ready, j + 2)
                    for k in range(KT):
                        ins = nc.tensor.transpose(tr[:, k], probs[:, k * P:(k + 1) * P], ident[:])
                    ins.then_inc(p_turned, 1)
                if p.out:
                    pe.wait_ge(p_lo_ready, j - 1)
                    pe.wait_ge(w_lo_ready, 2 * KT)
                    if p.post:
                        pe.wait_ge(x2_ready, j - 2)
                    for half in range(2):
                        ins = product(y_ps[:, half], p_hi[:, s], p_lo[:, s], b_hi, b_lo,
                                      slice(half * BANK, (half + 1) * BANK))
                    ins.then_inc(y_done, 1)

            turns(pe, body)

def ffn(nc, t):
    with Scope(nc, "ff") as c:
        BLOCKS = 2
        TB = SEQ // BLOCKS
        TT = TB // P
        CHUNKS = D_FF // (2 * P)
        RING = 4
        H0, FIRST = KT, 4
        TURN = 6
        turn_base = [H0 + FIRST]
        h_base = [0, turn_base[0] + TURN * CHUNKS]
        x_base = [h_base[1] + KT]
        turn_base.append(x_base[0] + TT)
        x_base.append(turn_base[1] + TURN * CHUNKS - FIRST)

        raw = c.sb("raw", [P, RING, D])
        h_hi, h_lo = c.sb("h_hi", [P, KT, TB], FR), c.sb("h_lo", [P, KT, TB], FR)
        gu_hi, gu_lo = c.sb("gu_hi", [P, 4, KT, P], FR), c.sb("gu_lo", [P, 4, KT, P], FR)
        wd_hi, wd_lo = c.sb("wd_hi", [P, 2, D], FR), c.sb("wd_lo", [P, 2, D], FR)
        act_hi, act_lo = c.sb("act_hi", [P, 2, 2, TB], FR), c.sb("act_lo", [P, 2, 2, TB], FR)
        y = c.sb("y", [P, TT, D])
        silu, hidden = c.sb("silu", [P, 2, BANK]), c.sb("hidden", [P, 2, BANK])
        gain = c.sb("gain", [P, D])
        ss, y0, tmp, rs = (c.sb(n, [P, TT]) for n in ("ss", "y0", "tmp", "rs"))
        gate_ps, up_ps, down_ps = c.ps("gate", [P, 2, BANK]), c.ps("up", [P, 2, BANK]), c.ps("down", [P, 4, BANK])
        ld, ld_gain = c.sems("ld", RING), c.sem("ld_gain")
        act_own, dve_own = c.sem("act_own"), c.sem("dve_own")
        hi_ready, lo_ready, gate_done, up_done, down_done = (
            c.sem(n) for n in ("hi_ready", "lo_ready", "gate_done", "up_done", "down_done"))
        silu_ready, hidden_ready, act_hi_ready, act_ready, added, guess, stored = (
            c.sem(n) for n in ("silu_ready", "hidden_ready", "act_hi_ready", "act_ready", "added", "guess", "stored"))
        block = c.enter_context(nc.Block())
        GROUPS = 2 * TT
        x2_d = t["x2"].rearrange("(t p) d -> t p d", p=P)
        out_d = t["out"].rearrange("(t p) d -> t p d", p=P)
        flat4 = lambda ap: ap.rearrange("p k n -> p (k n)")

        class Num:

            def __init__(self, base, i=0):
                self.base, self.i, self.slot = base, i, base % RING
                self.count = base + 12 * i + 1
                self.loads = base // RING + 1 + 3 * i
                self.first = isinstance(i, int) and base + 12 * i < RING

        def turns(eng, body, b, own=None, steps=0):
            body(0, 0, True, False)
            body(0, 1, True, True)
            with eng.Fori(1, CHUNKS // 2) as i:
                if own:
                    own.start(i - 1, steps)
                body(i, 0, True, True)
                body(i, 1, True, True)
            if own:
                own.end(CHUNKS // 2 - 1)
            body(CHUNKS // 2, 0, True, True)
            body(CHUNKS // 2, 1, False, True)

        def last_turn(i, e):
            return isinstance(i, int) and 2 * i + e == CHUNKS - 1

        def ring_turn(b, i, e):
            base = turn_base[b] + TURN * e
            gate_up = [] if b == BLOCKS - 1 and last_turn(i, e) else [Num(base + q, i) for q in range(4)]
            downs = [Num(base + len(gate_up) + q, i) for q in range(2)]
            return gate_up, downs

        @block.sync
        def _(sp):
            def load(n, src):
                if not n.first:
                    sp.wait_ge(lo_ready, n.count - RING)
                sp.dma_start(raw[:, n.slot], src).then_inc(ld[n.slot], 16)

            def load_gate_up(n, q, chunk):
                name, tile = ("w_gate", "w_up")[q % 2], 2 * chunk + q // 2
                load(n, t[name][tile].rearrange("p k n -> p (k n)"))

            def load_h(b):
                for k in range(KT):
                    load(Num(h_base[b] + k), t["h3_t"][k, :, b * TB:(b + 1) * TB])

            load_h(0)
            for q in range(4):
                load_gate_up(Num(H0 + q), q, 0)
            sp.dma_start(gain[:], rows_all(t["g_ffn_post"])).then_inc(ld_gain, 16)
            for b in range(BLOCKS):
                def body(i, e, gates, downs):
                    if not gates:
                        return
                    chunk = 2 * i + e
                    following = 0 if last_turn(i, e) else chunk + 1
                    gate_up, down = ring_turn(b, i, e)
                    for q, n in enumerate(gate_up):
                        load_gate_up(n, q, following)
                    for q, n in enumerate(down):
                        load(n, t["w_down"][bass.ds((2 * chunk + q) * P, P)])

                turns(sp, body, b)
                if b + 1 < BLOCKS:
                    load_h(b + 1)
                for i in range(TT):
                    load(Num(x_base[b] + i), x2_d[b * TT + i])
                for i in range(TT):
                    sp.wait_ge(lo_ready, Num(x_base[b] + i).count)
                    sp.dma_start(out_d[b * TT + i], y[:, i]).then_inc(stored, 16)
            sp.wait_ge(stored, 16 * NT)

        def split_hi(act, n, to, b):
            act.wait_ge(ld[n.slot], 16 * n.loads)
            nc.scalar.activation(to, raw[:, n.slot], ACT.Copy).then_inc(hi_ready, 1)

        def split_lo(dve, n, to, hi, b):
            dve.wait_ge(hi_ready, n.count - TT * b)
            nc.vector.tensor_tensor(to, raw[:, n.slot], hi.bitcast(F32), ALU.subtract).then_inc(lo_ready, 1)

        @block.scalar
        def _(act):
            own = Order(act, act_own)
            act.preload_act_table(ACT.Silu)
            for k in range(KT):
                split_hi(act, Num(k), h_hi[:, k], 0)
            for q in range(4):
                split_hi(act, Num(H0 + q), flat4(gu_hi[:, q]), 0)
            for b in range(BLOCKS):
                def body(i, e, gates, downs):
                    g = CHUNKS * b + 2 * i + e
                    if not gates:
                        if b + 1 < BLOCKS:
                            for k in range(KT):
                                split_hi(act, Num(h_base[b + 1] + k), h_hi[:, k], b)
                        return
                    gate_up, down = ring_turn(b, i, e)
                    for tile in range(2):
                        for half in range(2):
                            m = 4 * g + 2 * tile + half
                            early = isinstance(i, int) and b == 0 and i == 0 and e == 0 and tile == 0
                            act.wait_ge(gate_done, m + 1)
                            if not early:
                                at_least(act, hidden_ready, m - 1)
                            nc.scalar.activation(silu[:, half], gate_ps[:, half], ACT.Silu).then_inc(silu_ready, 1)
                            act.wait_ge(hidden_ready, m + 1)
                            if downs or b:
                                at_least(act, down_done, GROUPS * (g - 1))
                            nc.scalar.activation(act_hi[:, e, tile, half * BANK:(half + 1) * BANK], hidden[:, half],
                                                 ACT.Copy).then_inc(act_hi_ready, 1)
                        for q in (2 * tile, 2 * tile + 1):
                            if gate_up:
                                act.wait_ge(up_done, 4 * g + 2 * tile + 2)
                                split_hi(act, gate_up[q], flat4(gu_hi[:, q]), b)
                    if downs or b:
                        act.wait_ge(down_done, GROUPS * g)
                    for q in range(2):
                        split_hi(act, down[q], wd_hi[:, q], b)

                turns(act, body, b)
                act.wait_ge(added, GROUPS * CHUNKS * (b + 1))
                act.preload_act_table_set(LOG_EXP)
                for i in range(TT):
                    own.after(nc.scalar.activation(silu[:].rearrange("p a n -> p (a n)"), y[:, i], ACT.Square,
                                                   accum_out=ss[:, i:i + 1]))
                rsqrt_start(nc, own, y0[:], ss[:], 1.0 / D, EPS).then_inc(guess, 1)
                if b + 1 < BLOCKS:
                    act.preload_act_table(ACT.Silu)

        @block.vector
        def _(dve):
            own = Order(dve, dve_own)
            for k in range(KT):
                split_lo(dve, Num(k), h_lo[:, k], h_hi[:, k], 0)
            for q in range(4):
                split_lo(dve, Num(H0 + q), flat4(gu_lo[:, q]), flat4(gu_hi[:, q]), 0)
            dve.wait_ge(ld_gain, 16)
            for b in range(BLOCKS):
                def add(g, r, first):
                    dve.wait_ge(down_done, GROUPS * (g - 1) + r + 1)
                    to = y[:, r // 2, (r % 2) * BANK:(r % 2 + 1) * BANK]
                    if first:
                        if b:
                            dve.wait_ge(stored, 16 * TT * b)
                        nc.vector.tensor_copy(to, down_ps[:, r % 4]).then_inc(added, 1)
                    else:
                        nc.vector.tensor_tensor(to, down_ps[:, r % 4], to, ALU.add).then_inc(added, 1)

                def body(i, e, gates, downs):
                    g = CHUNKS * b + 2 * i + e
                    first = isinstance(i, int) and i == 0
                    if not gates:
                        for r in range(GROUPS):
                            add(g, r, False)
                            if b + 1 < BLOCKS and r % 2:
                                k = r // 2
                                split_lo(dve, Num(h_base[b + 1] + k), h_lo[:, k], h_hi[:, k], b)
                        return
                    gate_up, down = ring_turn(b, i, e)
                    for tile in range(2):
                        for half in range(2):
                            m = 4 * g + 2 * tile + half
                            at = (slice(None), e, tile, slice(half * BANK, (half + 1) * BANK))
                            dve.wait_ge(silu_ready, m + 1)
                            dve.wait_ge(up_done, m + 1)
                            nc.vector.tensor_tensor(hidden[:, half], up_ps[:, half], silu[:, half],
                                                    ALU.mult).then_inc(hidden_ready, 1)
                            dve.wait_ge(act_hi_ready, m + 1)
                            dve.wait_ge(hidden_ready, m + 1)
                            nc.vector.tensor_tensor(act_lo[at], hidden[:, half], act_hi[at].bitcast(F32),
                                                    ALU.subtract).then_inc(act_ready, 1)
                        for q in (2 * tile, 2 * tile + 1):
                            if gate_up:
                                split_lo(dve, gate_up[q], flat4(gu_lo[:, q]), flat4(gu_hi[:, q]), b)
                    if downs:
                        for r in range(GROUPS):
                            if not first:
                                dve.wait_ge(added, GROUPS * (g - 2) + r + 1)
                            add(g, r, first)
                    for q in range(2):
                        split_lo(dve, down[q], wd_lo[:, q], wd_hi[:, q], b)

                turns(dve, body, b)
                dve.wait_ge(guess, b + 1)
                own.after(rsqrt_end(nc, own, rs[:], y0[:], ss[:], tmp[:], 1.0 / D, EPS))
                for i in range(TT):
                    n = Num(x_base[b] + i)
                    own.after(nc.vector.scalar_tensor_tensor(y[:, i], y[:, i], rs[:, i:i + 1], gain[:], ALU.mult,
                                                             ALU.mult))
                    dve.wait_ge(ld[n.slot], 16 * n.loads)
                    nc.vector.tensor_tensor(y[:, i], y[:, i], raw[:, n.slot], ALU.add).then_inc(lo_ready, 1)

        @block.tensor
        def _(pe):
            for b in range(BLOCKS):
                def body(i, e, gates, downs):
                    g = CHUNKS * b + 2 * i + e
                    start = isinstance(i, int) and b == 0 and i == 0 and e == 0
                    if gates:
                        for tile in range(2):
                            if isinstance(i, int) and i == 0 and e == 0:
                                n = Num(H0 + 2 * tile + 1) if b == 0 else Num(turn_base[0] + TURN * (CHUNKS - 1) + 2 * tile + 1)
                                pe.wait_ge(lo_ready, n.count)
                                if b:
                                    pe.wait_ge(lo_ready, h_base[b] + KT)
                            else:
                                base = turn_base[b] + (0 if e else TURN - 12)
                                pe.wait_ge(lo_ready, Num(base + 2 * tile + 1, i).count)
                            for half in range(2):
                                m = 4 * g + 2 * tile + half
                                tok = slice(half * BANK, (half + 1) * BANK)
                                for ps, q, done, read in ((gate_ps, 2 * tile, gate_done, silu_ready),
                                                          (up_ps, 2 * tile + 1, up_done, hidden_ready)):
                                    if not (start and tile == 0):
                                        pe.wait_ge(read, m - 1)
                                    for k in range(KT):
                                        nc.tensor.matmul(ps[:, half], gu_hi[:, q, k], h_hi[:, k, tok],
                                                         start=(k == 0), stop=False)
                                        nc.tensor.matmul(ps[:, half], gu_hi[:, q, k], h_lo[:, k, tok],
                                                         start=False, stop=False)
                                        ins = nc.tensor.matmul(ps[:, half], gu_lo[:, q, k], h_hi[:, k, tok],
                                                               start=False, stop=(k == KT - 1))
                                    ins.then_inc(done, 1)
                    if downs:
                        base = turn_base[b] + (0 if e else -TURN) + 5
                        short = b == BLOCKS - 1 and not gates
                        pe.wait_ge(lo_ready, Num(base - (4 if short else 0), i).count)
                        pe.wait_ge(act_ready, 4 * g)
                        for r in range(GROUPS):
                            tok, n = slice((r // 2) * P, (r // 2 + 1) * P), slice((r % 2) * BANK, (r % 2 + 1) * BANK)
                            if not (isinstance(i, int) and b == 0 and i == 0 and r < 4):
                                pe.wait_ge(added, GROUPS * (g - 1) + r - 3)
                            for tile in range(2):
                                w = (wd_hi[:, tile, n], wd_lo[:, tile, n])
                                a_hi, a_lo = act_hi[:, 1 - e, tile, tok], act_lo[:, 1 - e, tile, tok]
                                nc.tensor.matmul(down_ps[:, r % 4], a_hi, w[0], start=(tile == 0), stop=False)
                                nc.tensor.matmul(down_ps[:, r % 4], a_hi, w[1], start=False, stop=False)
                                ins = nc.tensor.matmul(down_ps[:, r % 4], a_lo, w[0], start=False, stop=(tile == 1))
                            ins.then_inc(down_done, 1)

                turns(pe, body, b)

SCRATCH = {
    "a_mat": (D, D), "b_mat": (D, D), "pool_out": (4 * P, D),
    "proj": (PANELS, P, SEQ), "gate_rows": (2 * HEADS, SEQ), "chunk_ends": (HC, 2), "m_prev": (HEADS, NT),
    "neg_m": (HEADS, SEQ), "inter": (HEADS, SEQ), "decay": (HC,),
    "x1": (SEQ, D), "x2": (SEQ, D), "h3_t": (KT, P, SEQ),
}


def program(nc, t, stages=("memory_side", "mix", "cross", "ffn")):
    with Scope(nc, "all") as c:
        ident = c.sb("ident", [P, P])
        if "ident" in stages:
            i_sem = c.sem("i")
            with nc.Block() as b:
                @b.gpsimd
                def _(g):
                    make_identity(nc, g, i_sem, ident)
        if "memory_side" in stages:
            memory_side(nc, t, ident)
        if "mix" in stages:
            with Scope(nc, "mix") as mc:
                gate_rows = [mc.sb(n, [HC, P]) for n in ("gate_a", "gate_wk", "gate_en")]
                with Scope(nc, "h") as hc:
                    h_hi, h_lo = hc.sb("hi", [P, KT, SEQ], FR), hc.sb("lo", [P, KT, SEQ], FR)
                    mix_pre(nc, t, ident, h_hi, h_lo)
                    mix_in(nc, t, h_hi, h_lo, gate_rows)
                mlstm_out(nc, t, ident, gate_rows)
        if "cross" in stages:
            cross(nc, t, ident)
        if "ffn" in stages:
            ffn(nc, t)


def laid_out(i):
    import numpy as np

    f = lambda name: np.ascontiguousarray(i[name])[0]
    ins = {n: f(n) for n in (
        "x", "mem", "b_gate", "w_out", "g_mix_pre", "g_mix_post", "g_xattn_post", "g_ffn_post")}
    for name in ("g_mem", "g_xattn_pre", "pool_scale", "mlstm_norm_g", "g_ffn_pre"):
        ins[name + "_cols"] = f(name).reshape(-1, P).T
    ins["wk"], ins["wv"], ins["wo"] = f("wk_x"), f("wv_x"), f("wo_x")
    ins["wqt"] = f("wq_x").T
    ins["w_pool_t"] = f("w_pool").transpose(0, 2, 1)
    w_in = f("w_in")
    gates = np.zeros((D, P), w_in.dtype)
    gates[:, 0:HEADS] = w_in[:, 5 * BANK:5 * BANK + HEADS]
    gates[:, 32:32 + HEADS] = w_in[:, 5 * BANK + HEADS:5 * BANK + 2 * HEADS]
    w = np.concatenate([gates, w_in[:, BANK:5 * BANK], w_in[:, 0:BANK]], axis=1)
    ins["w_in"] = w.reshape(KT, P, PANELS, P).transpose(2, 1, 0, 3)
    conv = f("conv_qk")
    ins["conv"] = conv.reshape(4, KT, P).transpose(2, 1, 0)
    nf = D_FF // P
    for name in ("w_gate", "w_up"):
        ins[name] = f(name).reshape(KT, P, nf, P).transpose(2, 1, 0, 3)
    ins["w_down"] = f("w_down")
    return {k: np.ascontiguousarray(v) for k, v in ins.items()}


def kernel(**inputs):
    import numpy as np
    import concourse.bacc as bacc
    from concourse.bass_utils import run_bass_kernel_spmd

    nc = bacc.Bacc("TRN2", target_bir_lowering=False, num_devices=1)
    ins = laid_out(inputs)
    t = {k: nc.dram_tensor(f"in_{k}", v.shape, mybir.dt.from_np(v.dtype), kind="ExternalInput").ap()
         for k, v in ins.items()}
    for k, shape in SCRATCH.items():
        t[k] = nc.dram_tensor(f"scratch_{k}", shape, F32, kind="Internal").ap()
    t["out"] = nc.dram_tensor("out", (SEQ, D), F32, kind="ExternalOutput").ap()
    program(nc, t)
    r = run_bass_kernel_spmd(nc, [{f"in_{k}": v for k, v in ins.items()}], core_ids=[0])
    return r.results[0]["out"].reshape(1, SEQ, D)
```

```python
from contextlib import ExitStack

import concourse.bass as bass
from concourse import mybir

F32 = mybir.dt.float32
FR = mybir.dt.float32r
ACT = mybir.ActivationFunctionType
ALU = mybir.AluOpType
AX_X = mybir.AxisListType.X

P = 128
SEQ = 2048
D = 1024
KT = D // P
NT = SEQ // P
EPS = 1e-6
N_MEM = 256
HEADS = 4
DH = 128
X_DH = 256
POOL_WINDOWS = (2, 4, 8, 16)
D_FF = 2816
BANK = 512
NQ = SEQ // BANK
HC = HEADS * NT
PANELS = 21
Q0, K0, POOL0, O0, V0 = 1, 5, 9, 13, 17
HALO = 16
LOW = -1e30
LOG_EXP = "natural_log_exp_and_others"


class Scope(ExitStack):

    taken = set()

    def __init__(self, nc, tag):
        super().__init__()
        self.nc, self.tag = nc, tag

    def sb(self, name, shape, dt=F32):
        return self.enter_context(self.nc.sbuf_tensor(f"{self.tag}_{name}", shape, dt))

    def ps(self, name, shape, dt=F32):
        return self.enter_context(self.nc.psum_tensor(f"{self.tag}_{name}", shape, dt))

    def sem(self, name):
        sem = self.enter_context(self.nc.semaphore(f"{self.tag}_{name}"))
        assert sem.num not in self.taken, "out of semaphores"
        self.taken.add(sem.num)
        return sem

    def sems(self, name, n):
        return [self.sem(f"{name}{i}") for i in range(n)]


class Order:

    def __init__(self, sem):
        self.sem, self.base, self.n = sem, 0, 0

    def of(self, eng):
        self.eng = eng
        return self

    def after(self, ins):
        self.n += 1
        ins.then_inc(self.sem, 1)
        self.eng.wait_ge(self.sem, self.base + self.n)

    def start(self, i, per):
        self.kept = self.base + self.n
        self.base, self.n, self.per = self.kept + i * per, 0, per

    def end(self, turns):
        assert self.n == self.per, (self.n, self.per)
        self.base, self.n = self.kept + turns * self.per, 0


def at_least(eng, sem, n):
    if not isinstance(n, int) or n > 0:
        eng.wait_ge(sem, n)


def rows_all(vector):
    return vector.partition_broadcast(P)


def rsqrt_start(nc, order, y0, ss, scale, eps):
    order.after(nc.scalar.activation(y0, ss, ACT.Ln, scale=scale, bias=eps))
    return nc.scalar.activation(y0, y0, ACT.Exp, scale=-0.5)


def rsqrt_end(nc, order, out, y0, ss, tmp, scale, eps):
    order.after(nc.vector.tensor_scalar(tmp, ss, scale, eps, ALU.mult, ALU.add))
    order.after(nc.vector.tensor_tensor(tmp, tmp, y0, ALU.mult))
    order.after(nc.vector.tensor_tensor(tmp, tmp, y0, ALU.mult))
    order.after(nc.vector.tensor_scalar(tmp, tmp, -0.5, 1.5, ALU.mult, ALU.add))
    return nc.vector.tensor_tensor(out, tmp, y0, ALU.mult)


def rsqrt_end_act(nc, order, out, y0, ss, tmp, scale, eps):
    order.after(nc.scalar.activation(tmp, ss, ACT.Copy, scale=scale, bias=eps))
    order.after(nc.scalar.activation(tmp, tmp, ACT.Copy, scale=y0))
    order.after(nc.scalar.activation(tmp, tmp, ACT.Copy, scale=y0))
    order.after(nc.scalar.activation(tmp, tmp, ACT.Copy, scale=-0.5, bias=1.5))
    return nc.scalar.activation(out, tmp, ACT.Copy, scale=y0)


def make_identity(nc, g, sem, ident):
    g.memset(ident[:], 0.0).then_inc(sem, 1)
    g.wait_ge(sem, 1)
    g.affine_select(out=ident[:], in_=ident[:], compare_op=ALU.not_equal, fill=1.0, base=0,
                    pattern=[[-1, P]], channel_multiplier=1).then_inc(sem, 1)
    g.wait_ge(sem, 2)


def fold_and_norm(nc, t, act_own, dve_own, ident, h_hi, h_lo):
    with Scope(nc, "fn") as c:
        HALF = NT // 2
        gain = c.sb("gain", [P, D])
        x, h = c.sb("x", [P, 2, D]), c.sb("h", [P, 2, D])
        mem, mem_t = c.sb("mem", [P, 2, D]), c.sb("mem_t", [P, KT, N_MEM])
        kv_t = c.sb("kv_t", [P, KT, 2, N_MEM])
        w1, w2 = c.sb("w1", [P, 2, KT, P]), c.sb("w2", [P, 2, 2, D])
        w_out = kv_t[:].rearrange("p (r a) b m -> p r (a b m)", r=4)
        pool_t = w2[:, 0, 1, 0:BANK].rearrange("p (g c) -> p g c", g=4)
        stage_a, stage_b = mem, mem_t[:].rearrange("p (s k) m -> p s (k m)", s=2)
        wv = lambda s: w2[:, s, 0].rearrange("p (k n) -> p k n", k=KT)
        g_mem, g_q, pool_s = c.sb("g_mem", [P, KT]), c.sb("g_q", [P, KT]), c.sb("pool_s", [P, 4])
        m_ss, m_y0, m_tmp, m_rs = (c.sb("m_" + n, [P, 2]) for n in ("ss", "y0", "tmp", "rs"))
        ss, y0, tmp, rs = (c.sb(n, [P, 2]) for n in ("ss", "y0", "tmp", "rs"))
        acc = c.ps("acc", [P, 4, BANK])
        tr = c.ps("tr", [P, 2, KT, P])
        slot_row = lambda s: tr[:, s].rearrange("p k n -> p (k n)")
        bank_pair = lambda b: acc[:, b:b + 2].rearrange("p b n -> p (b n)")

        ld_mem, ld_small, ld_pool, ld_gain = (c.sem(n) for n in ("ld_mem", "ld_small", "ld_pool", "ld_gain"))
        ld_x, ld_w1, ld_w2 = (c.sems(n, 2) for n in ("ld_x", "ld_w1", "ld_w2"))
        stored_pool, stored = c.sem("stored_pool"), c.sems("stored", 2)
        ident_made, mem_guess, mem_normed, mem_turned, mem_t_ready, consts_ready = (
            c.sem(n) for n in ("ident_made", "mem_guess", "mem_normed", "mem_turned", "mem_t_ready", "consts_ready"))
        pool_done, pool_out, kv_done, kv_out, a_done, a_out, b_done, b_out = (
            c.sem(n) for n in ("pool_done", "pool_out", "kv_done", "kv_out", "a_done", "a_out", "b_done", "b_out"))
        guess, h_ready, turned, hi_ready, lo_ready = (
            c.sem(n) for n in ("guess", "h_ready", "turned", "hi_ready", "lo_ready"))
        block = c.enter_context(nc.Block())
        x_d = t["x"].rearrange("(t p) d -> t p d", p=P)

        def turns(eng, first_half, second_half, own=None, steps=0):
            for s in range(2):
                first_half(0, s)
            with eng.Fori(1, HALF // 2) as i:
                if own:
                    own.start(i - 1, steps)
                for s in range(2):
                    first_half(i, s)
            if own:
                own.end(HALF // 2 - 1)
            for n in range(HALF, NT):
                second_half(n, n % 2)

        @block.gpsimd
        def _(g):
            make_identity(nc, g, ident_made, ident)

        @block.sync
        def _(sp):
            def load_x(i, s):
                sp.dma_start(x[:, s], x_d[2 * i + s]).then_inc(ld_x[s], 16)

            def load_kv(i, s):
                sp.dma_start(w1[:, s], t["wk"][2 * i + s]).then_inc(ld_w1[s], 16)
                sp.dma_start(wv(s), t["wv"][2 * i + s]).then_inc(ld_w2[s], 16)

            sp.dma_start(mem[:], t["mem"].rearrange("(a p) d -> p a d", p=P)).then_inc(ld_mem, 16)
            sp.dma_start(g_mem[:], t["g_mem_cols"]).then_inc(ld_small, 16)
            sp.dma_start(g_q[:], t["g_xattn_pre_cols"]).then_inc(ld_small, 16)
            sp.dma_start(pool_s[:], t["pool_scale_cols"]).then_inc(ld_small, 16)
            sp.dma_start(pool_t, t["w_pool_t"].rearrange("g d c -> d g c")).then_inc(ld_pool, 16)
            sp.dma_start(w_out, t["w_out"][0:4 * P].rearrange("(k p) n -> p k n", p=P)).then_inc(ld_pool, 16)
            sp.dma_start(gain[:], rows_all(t["g_mix_pre"])).then_inc(ld_gain, 16)
            load_x(0, 0)
            load_kv(0, 0)
            load_x(0, 1)
            load_kv(0, 1)
            for r in range(4):
                sp.wait_ge(pool_out, r + 1)
                sp.dma_start(t["pool_out"][r * P:(r + 1) * P], w_out[:, r]).then_inc(stored_pool, 16)

            def next_x(i, s):
                sp.wait_ge(h_ready, 2 * i + s + 1)
                load_x(i + 1, s)

            def load_rest(i, s):
                sp.wait_ge(kv_done, 2 * i + s + 1)
                load_kv(i + 1, s)
                next_x(i, s)

            def load_wo(head):
                sp.dma_start(w2[:, head % 2], t["wo"][2 * head * P:(2 * head + 2) * P].rearrange("(k p) n -> p k n", p=P)
                             ).then_inc(ld_w2[head % 2], 16)

            for s in range(2):
                load_rest(0, s)
            with sp.Fori(1, HALF // 2 - 1) as i:
                for s in range(2):
                    load_rest(i, s)
            for s in range(2):
                sp.wait_ge(kv_done, HALF - 1 + s)
                sp.dma_start(w1[:, s], t["wqt"][s]).then_inc(ld_w1[s], 16)
                load_wo(s)
                next_x(HALF // 2 - 1, s)
            for n in range(HALF, NT):
                r, s = n - HALF, n % 2
                if n + 2 < NT:
                    sp.wait_ge(a_done, r + 1)
                    sp.dma_start(w1[:, s], t["wqt"][r + 2]).then_inc(ld_w1[s], 16)
                    next_x(n // 2, s)
                for out, stage, name in ((a_out, stage_a, "a_mat"), (b_out, stage_b, "b_mat")):
                    sp.wait_ge(out, r + 1)
                    sp.dma_start(t[name][r * P:(r + 1) * P], stage[:, s]).then_inc(stored[s], 16)
                if s and r // 2 + 2 < HEADS:
                    load_wo(r // 2 + 2)
            sp.wait_ge(stored_pool, 64)
            for s in range(2):
                sp.wait_ge(stored[s], 32 * (KT // 2))

        @block.scalar
        def _(act):
            own = act_own.of(act)
            act.preload_act_table_set(LOG_EXP)

            def stats(i, s):
                n = 2 * i + s
                act.wait_ge(ld_x[s], 16 * (i + 1))
                if not (isinstance(n, int) and n < 2):
                    act.wait_ge(turned, n - 1)
                own.after(nc.scalar.activation(h[:, s], x[:, s], ACT.Square, accum_out=ss[:, s:s + 1]))
                rsqrt_start(nc, own, y0[:, s:s + 1], ss[:, s:s + 1], 1.0 / D, EPS).then_inc(guess, 1)

            def high(tile, s):
                act.wait_ge(turned, tile + 1)
                nc.scalar.activation(h_hi[:, :, bass.ds(tile * P, P)], tr[:, s], ACT.Copy).then_inc(hi_ready, 1)

            def keep_kv(n, s):
                act.wait_ge(kv_done, n + 1)
                nc.scalar.activation(kv_t[:, bass.ds(n, 1)].rearrange("p o b m -> p (o b m)"), acc[:, s],
                                     ACT.Copy).then_inc(kv_out, 1)

            act.wait_ge(ld_mem, 16)
            for i in range(2):
                own.after(nc.scalar.activation(h[:, i], mem[:, i], ACT.Square, accum_out=m_ss[:, i:i + 1]))
            rsqrt_start(nc, own, m_y0[:], m_ss[:], 1.0 / D, EPS).then_inc(mem_guess, 1)
            stats(0, 0)
            act.wait_ge(ld_small, 48)
            for k in range(KT):
                act.wait_ge(mem_turned, k // 2 + 1)
                nc.scalar.activation(mem_t[:, k], acc[:, k // 2, (k % 2) * N_MEM:(k % 2 + 1) * N_MEM], ACT.Copy,
                                     scale=g_mem[:, k:k + 1]).then_inc(mem_t_ready, 1)

            def first_half(i, s):
                n = 2 * i + s
                if not (isinstance(n, int) and n == 0):
                    if isinstance(n, int) and n == 1:
                        act.wait_ge(stored_pool, 64)
                    keep_kv(n - 1, 1 - s)
                    high(n - 1, 1 - s)
                stats(i + s, 1 - s)

            def second_half(n, s):
                r = n - HALF
                if r == 0:
                    keep_kv(n - 1, 1 - s)
                high(n - 1, 1 - s)
                if n + 1 < NT:
                    stats((n + 1) // 2, 1 - s)
                act.wait_ge(a_done, r + 1)
                act.wait_ge(consts_ready, 1)
                if r >= 2:
                    act.wait_ge(stored[s], 32 * (r // 2))
                nc.scalar.activation(stage_a[:, s], bank_pair(0), ACT.Copy, scale=g_q[:, r:r + 1]).then_inc(a_out, 1)

            turns(act, first_half, second_half, own, 4)
            high(NT - 1, 1)

        @block.vector
        def _(dve):
            own = dve_own.of(dve)

            def normalise(n, s):
                dve.wait_ge(guess, n + 1)
                own.after(rsqrt_end(nc, own, rs[:, s:s + 1], y0[:, s:s + 1], ss[:, s:s + 1], tmp[:, s:s + 1],
                                    1.0 / D, EPS))
                nc.vector.scalar_tensor_tensor(h[:, s], x[:, s], rs[:, s:s + 1], gain[:], ALU.mult,
                                               ALU.mult).then_inc(h_ready, 1)

            def low(tile, s):
                dve.wait_ge(hi_ready, tile + 1)
                at = bass.ds(tile * P, P)
                nc.vector.tensor_tensor(h_lo[:, :, at], tr[:, s], h_hi[:, :, at].bitcast(F32),
                                        ALU.subtract).then_inc(lo_ready, 1)

            def keep_pool(r):
                dve.wait_ge(pool_done, r + 1)
                nc.vector.tensor_copy(w_out[:, r], slot_row(r % 2)).then_inc(pool_out, 1)

            dve.wait_ge(ld_small, 48)
            nc.vector.tensor_scalar(g_q[:], g_q[:], X_DH ** -0.5, None, ALU.mult).then_inc(consts_ready, 1)
            dve.wait_ge(mem_guess, 1)
            own.after(rsqrt_end(nc, own, m_rs[:], m_y0[:], m_ss[:], m_tmp[:], 1.0 / D, EPS))
            for i in range(2):
                nc.vector.tensor_scalar(mem[:, i], mem[:, i], m_rs[:, i:i + 1], None, ALU.mult).then_inc(mem_normed, 1)
            dve.wait_ge(ld_pool, 32)
            nc.vector.tensor_tensor(pool_t, pool_t, pool_s[:].unsqueeze(2).to_broadcast([P, 4, P]),
                                    ALU.mult).then_inc(consts_ready, 1)
            keep_pool(0)
            keep_pool(1)
            dve.wait_ge(ld_gain, 16)
            normalise(0, 0)
            keep_pool(2)
            keep_pool(3)

            def first_half(i, s):
                n = 2 * i + s
                if not (isinstance(n, int) and n == 0):
                    low(n - 1, 1 - s)
                normalise(n + 1, 1 - s)

            def second_half(n, s):
                r = n - HALF
                low(n - 1, 1 - s)
                if n + 1 < NT:
                    normalise(n + 1, 1 - s)
                dve.wait_ge(b_done, r + 1)
                if r >= 2:
                    dve.wait_ge(stored[s], 32 * (r // 2))
                nc.vector.tensor_copy(stage_b[:, s], bank_pair(2)).then_inc(b_out, 1)

            turns(dve, first_half, second_half, own, 10)
            low(NT - 1, 1)

        @block.tensor
        def _(pe):
            def pool(r):
                if r >= 2:
                    pe.wait_ge(pool_out, r - 1)
                for half in range(2):
                    n = slice(half * BANK, (half + 1) * BANK)
                    ins = nc.tensor.matmul(slot_row(r % 2)[:, n], pool_t[:, r], w_out[:, r, n], start=True, stop=True)
                ins.then_inc(pool_done, 1)

            def turn(tile, s):
                pe.wait_ge(h_ready, tile + 1)
                if isinstance(tile, int) and tile < 2:
                    pe.wait_ge(pool_out, 3 + tile)
                else:
                    pe.wait_ge(lo_ready, tile - 1)
                for k in range(KT):
                    ins = nc.tensor.transpose(tr[:, s, k], h[:, s, k * P:(k + 1) * P], ident[:])
                ins.then_inc(turned, 1)

            pe.wait_ge(ident_made, 2)
            pe.wait_ge(mem_normed, 2)
            for k in range(KT):
                for i in range(2):
                    at = (k % 2) * N_MEM + i * P
                    ins = nc.tensor.transpose(acc[:, k // 2, at:at + P], mem[:, i, k * P:(k + 1) * P], ident[:])
                if k % 2:
                    ins.then_inc(mem_turned, 1)
            pe.wait_ge(ld_pool, 32)
            pe.wait_ge(consts_ready, 2)
            for r in range(4):
                pool(r)
            pe.wait_ge(mem_t_ready, KT)

            def first_half(i, s):
                n = 2 * i + s
                if not (isinstance(n, int) and n < 2):
                    pe.wait_ge(kv_out, n - 1)
                for which, w, ld in ((0, w1[:, s], ld_w1[s]), (1, wv(s), ld_w2[s])):
                    pe.wait_ge(ld, 16 * (i + 1))
                    for k in range(KT):
                        ins = nc.tensor.matmul(acc[:, s, which * N_MEM:(which + 1) * N_MEM], w[:, k], mem_t[:, k],
                                               start=(k == 0), stop=(k == KT - 1))
                ins.then_inc(kv_done, 1)
                turn(n, s)

            def second_half(n, s):
                r = n - HALF
                if r == 0:
                    pe.wait_ge(kv_out, HALF)
                else:
                    pe.wait_ge(a_out, r)
                pe.wait_ge(ld_w1[s], 16 * (n // 2 + 1))
                for head in range(HEADS):
                    for dd in range(2):
                        ins = nc.tensor.matmul(acc[:, head // 2, (head % 2) * N_MEM:(head % 2 + 1) * N_MEM],
                                               w1[:, s, 2 * head + dd], kv_t[:, 2 * head + dd, 0],
                                               start=(dd == 0), stop=(dd == 1))
                ins.then_inc(a_done, 1)
                head, mm = divmod(r, 2)
                if r:
                    pe.wait_ge(b_out, r)
                pe.wait_ge(ld_w2[head % 2], 16 * (HALF // 2 + head // 2 + 1))
                for half in range(2):
                    for dd in range(2):
                        ins = nc.tensor.matmul(acc[:, 2 + half], kv_t[:, 2 * head + dd, 1, mm * P:(mm + 1) * P],
                                               w2[:, head % 2, dd, half * BANK:(half + 1) * BANK],
                                               start=(dd == 0), stop=(dd == 1))
                ins.then_inc(b_done, 1)
                turn(n, s)

            turns(pe, first_half, second_half)


def mix_in(nc, t, act_own, dve_own, h_hi, h_lo, gate_rows):
    with Scope(nc, "mi") as c:
        raw = c.sb("raw", [P, 2, KT, P])
        w_hi, w_lo = c.sb("w_hi", [P, 2, KT, P], FR), c.sb("w_lo", [P, 2, KT, P], FR)
        u = c.sb("u", [P, 2, HALO + SEQ])
        wa, wb = c.sb("wa", [P, HALO + SEQ]), c.sb("wb", [P, HALO + SEQ])
        res = c.sb("res", [P, 2, SEQ])
        taps = c.sb("taps", [P, KT, 4])
        bias = c.sb("bias", [P, 1])
        inv = c.sb("inv", [P, HALO])
        edge = c.sb("edge", [P, HALO])
        ga, gb, gi = gate_rows
        gf, gm, one = (c.sb(n, [HC, P]) for n in ("gf", "gm", "one"))
        ends = c.sb("ends", [HC, 2])
        heads = c.sb("heads", [HEADS, NT, 2])
        prev = c.sb("prev", [HEADS, NT + 1])
        m_prev = c.sb("m_prev", [HC, 1])
        acc = c.ps("acc", [P, 2, NQ, BANK])
        ld_w, ld_small, stored = c.sems("ld_w", 2), c.sem("ld_small"), c.sems("stored", 2)
        (consts, hi_ready, lo_ready, product, evacuated, conv_done, silu_done, pool_done) = (
            c.sem(n) for n in ("consts", "hi_ready", "lo_ready", "product", "evacuated", "conv_done",
                               "silu_done", "pool_done"))
        gates_out, gates_in, ends_ready, ends_out, ends_in, prev_ready, prev_out, prev_in = (
            c.sem(n) for n in ("gates_out", "gates_in", "ends_ready", "ends_out", "ends_in", "prev_ready",
                               "prev_out", "prev_in"))
        abs_ready, softplus_ready, neg_m_ready, exps_ready, gates_done, rows_out = (
            c.sem(n) for n in ("abs_ready", "softplus_ready", "neg_m_ready", "exps_ready", "gates_done", "rows_out"))
        block = c.enter_context(nc.Block())
        by_chunk = lambda name: t[name].rearrange("h (c l) -> (h c) l", l=P)
        flat = lambda s: acc[:, s].rearrange("p q n -> p (q n)")

        @block.gpsimd
        def _(g):
            nc.gpsimd.memset(bias[:], 0.0).then_inc(consts, 1)
            nc.gpsimd.memset(u[:, :, 0:HALO], 0.0).then_inc(consts, 1)
            nc.gpsimd.memset(one[:], 1.0).then_inc(consts, 1)
            nc.gpsimd.memset(prev[:, 0:1], 0.0).then_inc(consts, 1)
            for n in range(HALO):
                nc.gpsimd.memset(inv[:, n:n + 1], 1.0 / (n + 1)).then_inc(consts, 1)

        @block.sync
        def _(sp):
            def load(h, s):
                sp.dma_start(raw[:, s], t["w_in"][2 * h + s]).then_inc(ld_w[s], 16)

            def turn(h, s, ready, count, more=True):
                if more:
                    sp.wait_ge(lo_ready, 2 * h + s + 1)
                    load(h + 1, s)
                sp.wait_ge(ready, count)
                sp.dma_start(t["proj"][2 * h + s], res[:, s]).then_inc(stored[s], 16)

            load(0, 0)
            load(0, 1)
            sp.dma_start(taps[:], t["conv"]).then_inc(ld_small, 16)
            sp.wait_ge(consts, 1)
            b_gate = t["b_gate"].rearrange("(a d) -> a d", d=1)
            sp.dma_start(bias[0:HEADS], b_gate[0:HEADS]).then_inc(ld_small, 16)
            sp.dma_start(bias[32:32 + HEADS], b_gate[HEADS:2 * HEADS]).then_inc(ld_small, 16)
            sp.wait_ge(lo_ready, 1)
            load(1, 0)
            sp.wait_ge(evacuated, 1)
            for j in range(4):
                sp.dma_start(t["gate_rows"][j * HEADS:(j + 1) * HEADS],
                             res[32 * j:32 * j + HEADS, 0]).then_inc(gates_out, 16)
            sp.wait_ge(gates_out, 64)
            for j, to in enumerate((gi, gf, ga, gb)):
                sp.dma_start(to[:], by_chunk("gate_rows")[j * HC:(j + 1) * HC]).then_inc(gates_in, 16)
            sp.wait_ge(ends_ready, 2)
            sp.dma_start(t["chunk_ends"], ends[:]).then_inc(ends_out, 16)
            sp.wait_ge(ends_out, 16)
            sp.dma_start(heads[:], t["chunk_ends"].rearrange("(h c) e -> h c e", h=HEADS)).then_inc(ends_in, 16)
            sp.wait_ge(prev_ready, 1)
            sp.dma_start(t["m_prev"], prev[:, 0:NT]).then_inc(prev_out, 16)
            sp.wait_ge(prev_out, 16)
            sp.dma_start(m_prev[:], t["m_prev"].rearrange("h (c a) -> (h c) a", a=1)).then_inc(prev_in, 16)
            sp.wait_ge(neg_m_ready, 1)
            sp.dma_start(by_chunk("neg_m"), gm[:]).then_inc(rows_out, 16)
            sp.wait_ge(exps_ready, 3)
            sp.dma_start(by_chunk("inter"), gf[:]).then_inc(rows_out, 16)
            sp.dma_start(t["decay"].rearrange("(a d) -> a d", d=1), gf[:, P - 1:P]).then_inc(rows_out, 16)
            with sp.Fori(0, 4) as i:
                turn(i, 1, silu_done, 2 * i + 1)
                turn(i + 1, 0, silu_done, 2 * i + 2)
            for g in range(4):
                h, s = divmod(POOL0 + g, 2)
                turn(h, s, pool_done, g + 1)
            with sp.Fori(6, 9) as i:
                turn(i, 1, evacuated, 2 * i + 2)
                turn(i + 1, 0, evacuated, 2 * i + 3)
            turn(9, 1, evacuated, 20, more=False)
            turn(10, 0, evacuated, 21, more=False)
            sp.wait_ge(rows_out, 48)
            for s in range(2):
                sp.wait_ge(stored[s], 160)

        def res_free(eng, h, s):
            eng.wait_ge(gates_out, 64)
            at_least(eng, stored[s], 16 * (h if s else h - 1))

        @block.scalar
        def _(act):
            own = act_own.of(act)
            act.preload_act_table_set(LOG_EXP)

            def high(h, s):
                act.wait_ge(ld_w[s], 16 * (h + 1))
                nc.scalar.activation(w_hi[:, s], raw[:, s], ACT.Copy).then_inc(hi_ready, 1)

            def stage(h, s):
                act.wait_ge(product, 2 * h + s + 1)
                nc.scalar.activation(u[:, s, HALO:], flat(s), ACT.Copy).then_inc(evacuated, 1)

            high(0, 0)
            high(0, 1)
            act.wait_ge(product, 1)
            act.wait_ge(ld_small, 48)
            nc.scalar.activation(res[:, 0], flat(0), ACT.Identity, bias=bias[:]).then_inc(evacuated, 1)
            high(1, 0)
            act.wait_ge(abs_ready, 1)
            own.after(nc.scalar.activation(gb[:], ga[:], ACT.Exp, scale=-1.0))
            nc.scalar.activation(gb[:], gb[:], ACT.Ln, bias=1.0).then_inc(softplus_ready, 1)
            act.wait_ge(gates_done, 2)
            nc.scalar.activation(gb[:], ga[:], ACT.Exp, bias=gm[:, P - 1:P]).then_inc(exps_ready, 1)
            nc.scalar.activation(gi[:], gi[:], ACT.Exp).then_inc(exps_ready, 1)
            nc.scalar.activation(gf[:], gf[:], ACT.Exp).then_inc(exps_ready, 1)
            act.preload_act_table(ACT.Silu)

            def silu_panel(h, s, first=False):
                panel = 2 * h + s
                if not first:
                    act.wait_ge(conv_done, panel - 2)
                stage(h, s)
                high(h + 1, s)
                act.wait_ge(conv_done, panel)
                res_free(act, h, s)
                nc.scalar.activation(res[:, s], (wa if s else wb)[:, 0:SEQ], ACT.Silu).then_inc(silu_done, 1)

            silu_panel(0, 1, True)
            silu_panel(1, 0, True)
            with act.Fori(1, 4) as i:
                silu_panel(i, 1)
                silu_panel(i + 1, 0)

            for g in range(4):
                h, s = divmod(POOL0 + g, 2)
                if g >= 2:
                    act.wait_ge(pool_done, g - 1)
                stage(h, s)
                high(h + 1, s)

            def plain_panel(h, s, func, more=True):
                act.wait_ge(product, 2 * h + s + 1)
                res_free(act, h, s)
                nc.scalar.activation(res[:, s], flat(s), func).then_inc(evacuated, 1)
                if more:
                    high(h + 1, s)

            act.preload_act_table(ACT.Sigmoid)
            with act.Fori(6, 8) as i:
                plain_panel(i, 1, ACT.Sigmoid)
                plain_panel(i + 1, 0, ACT.Sigmoid)
            plain_panel(8, 1, ACT.Copy)
            plain_panel(9, 0, ACT.Copy)
            plain_panel(9, 1, ACT.Copy, more=False)
            plain_panel(10, 0, ACT.Copy, more=False)

        @block.vector
        def _(dve):
            own = dve_own.of(dve)

            def low(h, s):
                dve.wait_ge(hi_ready, 2 * h + s + 1)
                nc.vector.tensor_tensor(w_lo[:, s], raw[:, s], w_hi[:, s].bitcast(F32),
                                        ALU.subtract).then_inc(lo_ready, 1)

            dve.wait_ge(hi_ready, 1)
            nc.vector.tensor_tensor(w_hi[:, 0, :, P // 2:], raw[:, 0, :, P // 2:], w_hi[:, 0, :, P // 2:].bitcast(F32),
                                    ALU.subtract).then_inc(lo_ready, 1)
            low(0, 1)
            low(1, 0)
            dve.wait_ge(gates_in, 64)
            dve.wait_ge(consts, 4 + HALO)
            own.after(nc.vector.tensor_tensor(gf[:], gf[:], gb[:], ALU.add))
            own.after(nc.vector.tensor_tensor(gi[:], gi[:], ga[:], ALU.add))
            nc.vector.scalar_tensor_tensor(ga[:], gf[:], -1.0, gf[:], ALU.mult, ALU.max).then_inc(abs_ready, 1)
            dve.wait_ge(softplus_ready, 1)
            own.after(nc.vector.scalar_tensor_tensor(gf[:], gf[:], 0.0, gb[:], ALU.min, ALU.subtract))
            own.after(nc.vector.tensor_tensor_scan(gb[:], one[:], gf[:], 0.0, ALU.mult, ALU.add))
            own.after(nc.vector.tensor_tensor(ga[:], gi[:], gb[:], ALU.subtract))
            own.after(nc.vector.tensor_tensor_scan(gm[:], ga[:], ga[:], -3e38, ALU.max, ALU.max))
            nc.vector.tensor_copy(ends[:, 0:1], gm[:, P - 1:P]).then_inc(ends_ready, 1)
            nc.vector.tensor_copy(ends[:, 1:2], gb[:, P - 1:P]).then_inc(ends_ready, 1)
            dve.wait_ge(ends_in, 16)
            nc.vector.tensor_tensor_scan(prev[:, 1:], heads[:, :, 0], heads[:, :, 1], 0.0, ALU.max,
                                         ALU.add).then_inc(prev_ready, 1)
            dve.wait_ge(prev_in, 16)
            nc.vector.tensor_scalar(gm[:], gm[:], m_prev[:, 0:1], -1.0, ALU.max, ALU.mult).then_inc(neg_m_ready, 1)
            dve.wait_ge(neg_m_ready, 1)
            nc.vector.tensor_scalar(gf[:], gm[:], m_prev[:, 0:1], None, ALU.add).then_inc(gates_done, 1)
            nc.vector.tensor_tensor(gi[:], gm[:], gb[:], ALU.subtract).then_inc(gates_done, 1)

            dve.wait_ge(ld_small, 48)

            def conv_panel(h, s, first=False):
                panel = 2 * h + s
                low(h + 1, s)
                dve.wait_ge(evacuated, panel + 1)
                if not first:
                    dve.wait_ge(silu_done, panel - 2)
                to = (wa if s else wb)[:, 0:SEQ]
                tap = lambda n: (u[:, s, HALO - 3 + n:HALO - 3 + n + SEQ], taps[:, bass.ds(panel - 1, 1), n])
                own.after(nc.vector.tensor_scalar(to, tap(0)[0], tap(0)[1], None, ALU.mult))
                for n in range(1, 4):
                    ins = nc.vector.scalar_tensor_tensor(to, tap(n)[0], tap(n)[1], to, ALU.mult, ALU.add)
                    if n < 3:
                        own.after(ins)
                ins.then_inc(conv_done, 1)

            conv_panel(0, 1, True)
            conv_panel(1, 0, True)
            with dve.Fori(1, 4) as i:
                own.start(i - 1, 6)
                conv_panel(i, 1)
                conv_panel(i + 1, 0)
            own.end(3)
            dve.wait_ge(silu_done, 8)
            for g, window in enumerate(POOL_WINDOWS):
                h, s = divmod(POOL0 + g, 2)
                low(h + 1, s)
                dve.wait_ge(evacuated, 2 * h + s + 1)
                at, total, other, step = 1, u[:, s], wa, 1
                while step < window:
                    own.after(nc.vector.tensor_tensor(other[:, at:], total[:, at:],
                                                      total[:, at - step:HALO + SEQ - step], ALU.add))
                    total, other = other, (wb if other is wa else wa)
                    step *= 2
                    at += step
                res_free(dve, h, s)
                own.after(nc.vector.scalar_tensor_tensor(res[:, s], total[:, HALO:], 1.0 / window, u[:, s, HALO:],
                                                         ALU.mult, ALU.subtract))
                own.after(nc.vector.tensor_tensor(edge[:], total[:, HALO:2 * HALO], inv[:], ALU.mult))
                nc.vector.tensor_tensor(res[:, s, 0:window - 1], edge[:, 0:window - 1],
                                        u[:, s, HALO:HALO + window - 1], ALU.subtract).then_inc(pool_done, 1)
            with dve.Fori(6, 9) as i:
                low(i + 1, 1)
                low(i + 2, 0)

        @block.tensor
        def _(pe):
            def panel(h, s, first=False):
                pe.wait_ge(lo_ready, 2 * h + s + 1)
                if not first:
                    at_least(pe, evacuated, 2 * h + s - 1)
                for q in range(NQ):
                    at = slice(q * BANK, (q + 1) * BANK)
                    for k in range(KT):
                        nc.tensor.matmul(acc[:, s, q], w_hi[:, s, k], h_hi[:, k, at], start=(k == 0), stop=False)
                        nc.tensor.matmul(acc[:, s, q], w_hi[:, s, k], h_lo[:, k, at], start=False, stop=False)
                        last = nc.tensor.matmul(acc[:, s, q], w_lo[:, s, k], h_hi[:, k, at], start=False,
                                                stop=(k == KT - 1))
                last.then_inc(product, 1)

            pe.wait_ge(lo_ready, 1)
            for q in range(NQ):
                at = slice(q * BANK, (q + 1) * BANK)
                for k in range(KT):
                    nc.tensor.matmul(acc[:, 0, q], w_hi[:, 0, k], h_hi[:, k, at], start=(k == 0), stop=False)
                    last = nc.tensor.matmul(acc[:, 0, q], w_hi[:, 0, k], h_lo[:, k, at], start=False,
                                            stop=(k == KT - 1))
            last.then_inc(product, 1)
            panel(0, 1, True)
            panel(1, 0)
            with pe.Fori(1, 10) as i:
                panel(i, 1)
                panel(i + 1, 0)


def mlstm_out(nc, t, act_own, dve_own, ident, gate_rows):
    with Scope(nc, "mo") as c:
        DA = DH + 1
        raw = c.sb("raw", [P, KT, D])
        w_hi, w_lo = c.sb("w_hi", [P, KT, D], FR), c.sb("w_lo", [P, KT, D], FR)
        w_gain = c.sb("w_gain", [P, KT])
        gain = c.sb("gain", [P, D])
        qkv, od = c.sb("qkv", [P, 2, 3, HEADS, P]), c.sb("od", [P, 2, 2, HEADS, P])
        neg_m, inter = c.sb("neg_m", [P, 2, HEADS, P]), c.sb("inter", [P, 2, HEADS, P])
        cols, decay = c.sb("cols", [P, 3, HEADS, NT]), c.sb("decay", [P, HEADS, NT])
        cap = c.sb("cap", [P, P])
        probs, scores, qs = (c.sb(n, [P, HEADS, P]) for n in ("probs", "scores", "qs"))
        vn, kn = c.sb("vn", [P, HEADS, DA]), c.sb("kn", [P, HEADS, DH])
        state = c.sb("state", [P, HEADS, DA])
        heads = c.sb("heads", [P, HEADS, DH])
        gated = c.sb("gated", [P, HEADS, P])
        mix_hi, mix_lo = c.sb("mix_hi", [P, 2, KT, P], FR), c.sb("mix_lo", [P, 2, KT, P], FR)
        x, x1 = c.sb("x", [P, 2, D]), c.sb("x1", [P, 2, D])
        normed, junk = c.sb("normed", [P, D]), c.sb("junk", [P, D])
        h_ss, h_y0, h_tmp, h_rs, den, h_var = (c.sb(n, [P, HEADS]) for n in ("h_ss", "h_y0", "h_tmp", "h_rs", "den", "h_var"))
        y_ss, y_y0, y_tmp, y_rs = (c.sb(n, [P, 1]) for n in ("y_ss", "y_y0", "y_tmp", "y_rs"))
        turn_ps = c.ps("turn", [P, HEADS, P])
        kv_ps = c.ps("kv", [P, 2, BANK])
        s_ps = c.ps("s", [P, HEADS, P])
        n_ps = c.ps("n", [P, 2, BANK])
        y_ps = c.ps("y", [P, 2, BANK])
        k_turn_ps = kv_ps[:, 0].rearrange("p (h e) -> p h e", h=HEADS)
        pairs = lambda ps: ps[:, :, 0:2 * DA].rearrange("p b (h e) -> p b h e", h=2)
        one_head = lambda ps, h, n: ps[:, h // 2, (h % 2) * DA:(h % 2) * DA + n]
        by_pair = lambda ap: ap.rearrange("p (b h) e -> p b h e", b=2)
        two = lambda ap: ap.rearrange("p (b h) -> p b h", b=2)

        ld_w, ld_const, ld_gain = c.sems("ld_w", KT // 2), c.sem("ld_const"), c.sem("ld_gain")
        ld_qkv, ld_bc, ld_od, ld_x = (c.sems(n, 2) for n in ("ld_qkv", "ld_bc", "ld_od", "ld_x"))
        stored = c.sems("stored", 2)
        consts, w_hi_ready, w_lo_ready, cols_turned, cols_ready = (
            c.sem(n) for n in ("consts", "w_hi_ready", "w_lo_ready", "cols_turned", "cols_ready"))
        v_turned, k_turned, s_done, n_done, kv_done, m_turned, y_done = (
            c.sem(n) for n in ("v_turned", "k_turned", "s_done", "n_done", "kv_done", "m_turned", "y_done"))
        vn_ready, probs_ready, squares, h_guess, d_hi, m_hi, y_guess = (
            c.sem(n) for n in ("vn_ready", "probs_ready", "squares", "h_guess", "d_hi", "m_hi", "y_guess"))
        args_ready, kn_ready, qs_ready, scores_ready, var_ready, heads_ready, gated_ready = (
            c.sem(n) for n in ("args_ready", "kn_ready", "qs_ready", "scores_ready", "var_ready", "heads_ready",
                               "gated_ready"))
        mix_ready, y_read, x1_ready, state_ready = (c.sem(n) for n in ("mix_ready", "y_read", "x1_ready", "state_ready"))
        block = c.enter_context(nc.Block())

        x_d = t["x"].rearrange("(t p) d -> t p d", p=P)
        x1_d = t["x1"].rearrange("(t p) d -> t p d", p=P)
        chunk = lambda lo, hi, cc: t["proj"][lo:hi, :, bass.ds(cc * P, P)].rearrange("h p l -> p h l")

        def turns(eng, body, own=None, steps=0):
            body(0, 0, True, False, False)
            body(0, 1, True, True, False)
            body(1, 0, True, True, True)
            body(1, 1, True, True, True)
            with eng.Fori(2, NT // 2) as i:
                if own:
                    own.start(i - 2, steps)
                body(i, 0, True, True, True)
                body(i, 1, True, True, True)
            if own:
                own.end(NT // 2 - 2)
            body(NT // 2, 0, False, True, True)
            body(NT // 2, 1, False, False, True)

        @block.gpsimd
        def _(g):
            nc.gpsimd.memset(w_gain[:, 0:4], 1.0).then_inc(consts, 1)
            nc.gpsimd.memset(vn[:, :, DH:], 1.0).then_inc(consts, 1)
            nc.gpsimd.memset(state[:], 0.0).then_inc(consts, 1)
            nc.gpsimd.memset(cap[:], 0.0).then_inc(consts, 1)
            g.wait_ge(consts, 4)
            nc.gpsimd.affine_select(out=cap[:], in_=cap[:], compare_op=ALU.is_ge, fill=LOW, base=0,
                                    pattern=[[1, P]], channel_multiplier=-1).then_inc(consts, 1)

        @block.sync
        def _(sp):
            def load_w(k):
                src = t["pool_out"][k * P:(k + 1) * P] if k < 4 else t["w_out"][k * P:(k + 1) * P]
                sp.dma_start(raw[:, k], src).then_inc(ld_w[k // 2], 16)

            def load_chunk(cc, s):
                for j, panel in enumerate((Q0, K0, V0)):
                    sp.dma_start(qkv[:, s, j], chunk(panel, panel + 4, cc)).then_inc(ld_qkv[s], 16)
                for to, name in ((neg_m, "neg_m"), (inter, "inter")):
                    sp.dma_start(to[:, s], t[name][:, bass.ds(cc * P, P)].partition_broadcast(P)).then_inc(ld_bc[s], 16)

            def load_od(cc, s):
                for j, panel in enumerate((O0, POOL0)):
                    sp.dma_start(od[:, s, j], chunk(panel, panel + 4, cc)).then_inc(ld_od[s], 16)

            load_chunk(0, 0)
            sp.dma_start(decay[:].rearrange("p h c -> p (h c)"), t["decay"].partition_broadcast(P)).then_inc(ld_const, 16)
            sp.dma_start(w_gain[:, 4:], t["mlstm_norm_g_cols"]).then_inc(ld_const, 16)
            load_chunk(1, 1)
            load_od(0, 0)
            for k in range(KT):
                load_w(k)
            sp.dma_start(gain[:], rows_all(t["g_mix_post"])).then_inc(ld_gain, 16)

            def body(h, s, now, before, out):
                cc = 2 * h + s
                if now:
                    if out:
                        sp.wait_ge(mix_ready, cc - 1)
                    if not (isinstance(cc, int) and cc == 0):
                        load_od(cc, s)
                    sp.dma_start(x[:, s], x_d[cc]).then_inc(ld_x[s], 16) if not out else None
                if out:
                    sp.wait_ge(x1_ready, cc - 1)
                    sp.dma_start(x1_d[cc - 2], x1[:, s]).then_inc(stored[s], 16)
                    if now:
                        sp.dma_start(x[:, s], x_d[cc]).then_inc(ld_x[s], 16)

            def ahead(h, s):
                cc = 2 * h + s
                sp.wait_ge(k_turned, cc + 1)
                sp.wait_ge(qs_ready, cc + 1)
                load_chunk(cc + 2, s)

            for cc in range(4):
                body(cc // 2, cc % 2, True, cc > 0, cc > 1)
                ahead(cc // 2, cc % 2)
            with sp.Fori(2, NT // 2 - 1) as i:
                for s in range(2):
                    body(i, s, True, True, True)
                    ahead(i, s)
            body(NT // 2 - 1, 0, True, True, True)
            body(NT // 2 - 1, 1, True, True, True)
            body(NT // 2, 0, False, True, True)
            body(NT // 2, 1, False, False, True)
            for s in range(2):
                sp.wait_ge(stored[s], 16 * (NT // 2))

        @block.scalar
        def _(act):
            own = act_own.of(act)
            act.preload_act_table_set(LOG_EXP)
            act.wait_ge(cols_turned, 1)
            nc.scalar.activation(cols[:].rearrange("p k h c -> p (k h c)"),
                                 turn_ps[:].rearrange("p h e -> p (h e)")[:, 0:3 * HC], ACT.Copy).then_inc(cols_ready, 1)
            act.wait_ge(ld_const, 32)
            act.wait_ge(consts, 1)

            def body(h, s, now, before, out):
                cc = 2 * h + s
                if now:
                    act.wait_ge(v_turned, cc + 1)
                    if before:
                        act.wait_ge(kv_done, cc)
                    nc.scalar.activation(vn[:, :, 0:DH], turn_ps[:], ACT.Copy).then_inc(vn_ready, 1)
                    act.wait_ge(args_ready, cc + 1)
                    nc.scalar.activation(probs[:], probs[:], ACT.Exp).then_inc(probs_ready, 1)
                if before:
                    act.wait_ge(n_done, cc)
                    for hd in range(HEADS):
                        ins = nc.scalar.activation(junk[:, hd * DH:(hd + 1) * DH], one_head(n_ps, hd, DH), ACT.Square,
                                                   accum_out=h_ss[:, hd:hd + 1])
                    ins.then_inc(squares, 1)
                    act.wait_ge(var_ready, cc)
                    rsqrt_start(nc, own, h_y0[:], h_var[:], 1.0 / DH, EPS).then_inc(h_guess, 1)
                    act.wait_ge(ld_od[1 - s], 32 * (h + s))
                    if out:
                        at_least(act, y_done, cc - 2)
                    nc.scalar.activation(mix_hi[:, 1 - s, 0:4], od[:, 1 - s, 1], ACT.Copy).then_inc(d_hi, 1)
                if out:
                    act.wait_ge(y_done, cc - 1)
                    own.after(nc.scalar.activation(junk[:], y_ps[:].rearrange("p a n -> p (a n)"), ACT.Square,
                                                   accum_out=y_ss[:]))
                    rsqrt_start(nc, own, y_y0[:], y_ss[:], 1.0 / D, EPS).then_inc(y_guess, 1)
                if before:
                    act.wait_ge(gated_ready, cc)
                    nc.scalar.activation(mix_hi[:, 1 - s, 4:], gated[:], ACT.Copy).then_inc(m_hi, 1)
                if before and not out:
                    for k in range(KT):
                        act.wait_ge(ld_w[k // 2], 32)
                        nc.scalar.activation(w_hi[:, k], raw[:, k], ACT.Copy,
                                             scale=w_gain[:, k:k + 1]).then_inc(w_hi_ready, 1)

            turns(act, body, own, 6)

        @block.vector
        def _(dve):
            own = dve_own.of(dve)
            dve.wait_ge(ld_const, 32)
            dve.wait_ge(consts, 5)
            dve.wait_ge(cols_ready, 1)

            def body(h, s, now, before, out):
                cc = 2 * h + s
                at = bass.ds(cc, 1)
                if now:
                    dve.wait_ge(ld_bc[s], 32 * (h + 1))
                    for hd in range(HEADS):
                        ins = nc.vector.scalar_tensor_tensor(probs[:, hd], neg_m[:, s, hd], cols[:, 0, hd, at], cap[:],
                                                             ALU.add, ALU.min)
                    ins.then_inc(args_ready, 1)
                    dve.wait_ge(k_turned, cc + 1)
                    if before:
                        dve.wait_ge(kv_done, cc)
                    nc.vector.tensor_tensor(kn[:], k_turn_ps, cols[:, 1, :, at].to_broadcast([P, HEADS, DH]),
                                            ALU.mult).then_inc(kn_ready, 1)
                    nc.vector.scalar_tensor_tensor(qs[:], inter[:, s], DH ** -0.5, qkv[:, s, 0], ALU.mult,
                                                   ALU.mult).then_inc(qs_ready, 1)
                    dve.wait_ge(s_done, cc + 1)
                    dve.wait_ge(probs_ready, cc + 1)
                    nc.vector.scalar_tensor_tensor(scores[:], s_ps[:], DH ** -0.5, probs[:], ALU.mult,
                                                   ALU.mult).then_inc(scores_ready, 1)
                if before:
                    last = bass.ds(cc - 1, 1)
                    dve.wait_ge(squares, cc)
                    own.after(nc.vector.tensor_tensor(two(den[:]), pairs(n_ps)[:, :, :, DH],
                                                      two(cols[:, 2, :, last].rearrange("p h a -> p (h a)")), ALU.max))
                    own.after(nc.vector.scalar_tensor_tensor(two(den[:]), pairs(n_ps)[:, :, :, DH], -1.0, two(den[:]),
                                                             ALU.mult, ALU.max))
                    own.after(nc.vector.reciprocal(den[:], den[:]))
                    own.after(nc.vector.tensor_tensor(h_var[:], h_ss[:], den[:], ALU.mult))
                    nc.vector.tensor_tensor(h_var[:], h_var[:], den[:], ALU.mult).then_inc(var_ready, 1)
                    dve.wait_ge(h_guess, cc)
                    own.after(rsqrt_end(nc, own, h_rs[:], h_y0[:], h_var[:], h_tmp[:], 1.0 / DH, EPS))
                    own.after(nc.vector.tensor_tensor(h_rs[:], h_rs[:], den[:], ALU.mult))
                    if out:
                        dve.wait_ge(m_turned, cc - 1)
                    nc.vector.tensor_tensor(by_pair(heads[:]), pairs(n_ps)[:, :, :, 0:DH],
                                            two(h_rs[:]).unsqueeze(3).to_broadcast([P, 2, 2, DH]),
                                            ALU.mult).then_inc(heads_ready, 1)
                    dve.wait_ge(d_hi, cc)
                    nc.vector.tensor_tensor(mix_lo[:, 1 - s, 0:4], od[:, 1 - s, 1], mix_hi[:, 1 - s, 0:4].bitcast(F32),
                                            ALU.subtract)
                    dve.wait_ge(m_turned, cc)
                    nc.vector.tensor_tensor(gated[:], turn_ps[:], od[:, 1 - s, 0], ALU.mult).then_inc(gated_ready, 1)
                if out:
                    dve.wait_ge(y_guess, cc - 1)
                    if isinstance(cc, int) and cc == 2:
                        dve.wait_ge(ld_gain, 16)
                    own.after(rsqrt_end(nc, own, y_rs[:], y_y0[:], y_ss[:], y_tmp[:], 1.0 / D, EPS))
                    nc.vector.scalar_tensor_tensor(normed[:], y_ps[:].rearrange("p a n -> p (a n)"), y_rs[:],
                                                   gain[:], ALU.mult, ALU.mult).then_inc(y_read, 1)
                if before:
                    dve.wait_ge(m_hi, cc)
                    nc.vector.tensor_tensor(mix_lo[:, 1 - s, 4:], gated[:], mix_hi[:, 1 - s, 4:].bitcast(F32),
                                            ALU.subtract).then_inc(mix_ready, 1)
                if now:
                    dve.wait_ge(kv_done, cc + 1)
                    for hd in range(HEADS):
                        ins = nc.vector.scalar_tensor_tensor(state[:, hd], state[:, hd], decay[:, hd, at],
                                                             one_head(kv_ps, hd, DA), ALU.mult, ALU.add)
                    ins.then_inc(state_ready, 1)
                if before and not out:
                    for k in range(KT):
                        dve.wait_ge(w_hi_ready, k + 1)
                        nc.vector.scalar_tensor_tensor(w_lo[:, k], raw[:, k], w_gain[:, k:k + 1],
                                                       w_hi[:, k].bitcast(F32), ALU.mult,
                                                       ALU.subtract).then_inc(w_lo_ready, 1)
                if out:
                    dve.wait_ge(y_read, cc - 1)
                    dve.wait_ge(ld_x[s], 16 * h)
                    at_least(dve, stored[s], 16 * (h - 1))
                    nc.vector.tensor_tensor(x1[:, s], normed[:], x[:, s], ALU.add).then_inc(x1_ready, 1)

            turns(dve, body, own, 30)

        @block.tensor
        def _(pe):
            for j, rows in enumerate((gate_rows[0], gate_rows[1], gate_rows[2])):
                ins = nc.tensor.transpose(turn_ps[:].rearrange("p h e -> p (h e)")[:, j * HC:(j + 1) * HC], rows[:],
                                          ident[0:HC, 0:HC])
            ins.then_inc(cols_turned, 1)
            pe.wait_ge(cols_ready, 1)

            def body(h, s, now, before, out):
                cc = 2 * h + s
                if now:
                    pe.wait_ge(ld_qkv[s], 48 * (h + 1))
                    if out:
                        pe.wait_ge(gated_ready, cc - 1)
                    for hd in range(HEADS):
                        ins = nc.tensor.transpose(turn_ps[:, hd], qkv[:, s, 2, hd], ident[:])
                    ins.then_inc(v_turned, 1)
                    if before:
                        pe.wait_ge(scores_ready, cc)
                    for hd in range(HEADS):
                        ins = nc.tensor.matmul(s_ps[:, hd], qkv[:, s, 1, hd], qkv[:, s, 0, hd], start=True, stop=True)
                    ins.then_inc(s_done, 1)
                if out:
                    pe.wait_ge(mix_ready, cc - 1)
                    at_least(pe, y_read, cc - 2)
                    first_out = isinstance(cc, int) and cc == 2
                for half in range(2):
                    if half and now:
                        if before:
                            pe.wait_ge(state_ready, cc)
                        for hd in range(HEADS):
                            ins = nc.tensor.transpose(k_turn_ps[:, hd], qkv[:, s, 1, hd], ident[:])
                        ins.then_inc(k_turned, 1)
                    if out:
                        n = slice(half * BANK, (half + 1) * BANK)
                        for k in range(KT):
                            if first_out and half == 0:
                                pe.wait_ge(w_lo_ready, k + 1)
                            nc.tensor.matmul(y_ps[:, half], mix_hi[:, s, k], w_hi[:, k, n], start=(k == 0), stop=False)
                            nc.tensor.matmul(y_ps[:, half], mix_hi[:, s, k], w_lo[:, k, n], start=False, stop=False)
                            ins = nc.tensor.matmul(y_ps[:, half], mix_lo[:, s, k], w_hi[:, k, n], start=False,
                                                   stop=(k == KT - 1))
                        if half:
                            ins.then_inc(y_done, 1)
                if before:
                    pe.wait_ge(heads_ready, cc)
                    if now:
                        pe.wait_ge(vn_ready, cc + 1)
                    for hd in range(HEADS):
                        ins = nc.tensor.transpose(turn_ps[:, hd], heads[:, hd], ident[:])
                    ins.then_inc(m_turned, 1)
                if now:
                    pe.wait_ge(vn_ready, cc + 1)
                    pe.wait_ge(scores_ready, cc + 1)
                    pe.wait_ge(kn_ready, cc + 1)
                    for hd in range(HEADS):
                        nc.tensor.matmul(one_head(n_ps, hd, DA), scores[:, hd], vn[:, hd], start=True, stop=False)
                        ins = nc.tensor.matmul(one_head(n_ps, hd, DA), qs[:, hd], state[:, hd], start=False, stop=True)
                    ins.then_inc(n_done, 1)
                    for hd in range(HEADS):
                        ins = nc.tensor.matmul(one_head(kv_ps, hd, DA), kn[:, hd], vn[:, hd], start=True, stop=True)
                    ins.then_inc(kv_done, 1)

            turns(pe, body)

def cross(nc, t, act_own, dve_own, ident):
    with Scope(nc, "cr") as c:
        a_hi, a_lo = c.sb("a_hi", [P, KT, D], FR), c.sb("a_lo", [P, KT, D], FR)
        b_hi, b_lo = c.sb("b_hi", [P, KT, D], FR), c.sb("b_lo", [P, KT, D], FR)
        RAW = 4
        raw = c.sb("raw", [P, RAW, D])
        x2, xb, h3 = raw[:, 0:2], raw[:, 2], raw[:, 3]
        xa = c.sb("xa", [P, 2, D])
        h_buffer, probs = c.sb("h", [P, D]), c.sb("probs", [P, D])
        junk, gain = c.sb("junk", [P, D]), c.sb("gain", [P, D])
        g_ffn = c.sb("g_ffn", [P, KT])
        h_hi, h_lo = c.sb("h_hi", [P, 2, KT, P], FR), c.sb("h_lo", [P, 2, KT, P], FR)
        p_hi, p_lo = c.sb("p_hi", [P, 2, KT, P], FR), c.sb("p_lo", [P, 2, KT, P], FR)
        h3_t = c.sb("h3_t", [P, KT, P])
        x_st, y_st, z_st = ([c.sb(a + n, [P, 1]) for n in ("ss", "y0", "tmp", "rs")] for a in ("x_", "y_", "z_"))
        neg_max, sums = c.sb("neg_max", [P, HEADS]), c.sb("sums", [P, HEADS])
        s_ps, y_ps = c.ps("s", [P, 2, BANK]), c.ps("y", [P, 2, BANK])
        tr, tr3 = c.ps("tr", [P, KT, P]), c.ps("tr3", [P, KT, P])
        flat = lambda ps: ps[:].rearrange("p a n -> p (a n)")
        out_ps = lambda p: s_ps if p.j == NT + 1 else y_ps
        by_head = lambda ap: ap.rearrange("p (h m) -> p h m", h=HEADS)

        ld_w, ld_const, ld_xa, ld_xb = c.sems("ld_w", RAW), c.sem("ld_const"), c.sems("ld_xa", 2), c.sem("ld_xb")
        stored, stored3 = c.sems("stored", 2), c.sem("stored3")
        w_hi_ready, w_lo_ready = c.sem("w_hi_ready"), c.sem("w_lo_ready")
        x_guess, y_guess, z_guess, h_hi_ready, p_hi_ready, exps = (
            c.sem(n) for n in ("x_guess", "y_guess", "z_guess", "h_hi_ready", "p_hi_ready", "exps"))
        h_ready, h_lo_ready, max_ready, probs_ready, p_lo_ready, x2_ready, h3_ready, h3_t_ready = (
            c.sem(n) for n in ("h_ready", "h_lo_ready", "max_ready", "probs_ready", "p_lo_ready", "x2_ready",
                               "h3_ready", "h3_t_ready"))
        h_turned, p_turned, x_turned, s_done, y_done = (
            c.sem(n) for n in ("h_turned", "p_turned", "x_turned", "s_done", "y_done"))
        block = c.enter_context(nc.Block())
        tiles = lambda name: t[name].rearrange("(t p) d -> t p d", p=P)

        class Parts:

            def __init__(self, j=None):
                inner = j is None
                self.scores = inner or j < NT
                self.ahead = inner or j + 1 < NT
                self.ahead2 = inner or j + 2 < NT
                self.probs = inner or 1 <= j <= NT
                self.out = inner or 2 <= j <= NT + 1
                self.post = inner or 3 <= j
                self.j = j

        def turns(eng, body, own=None, steps=0):
            for j in range(6):
                body(j // 2, j % 2, Parts(j))
            with eng.Fori(3, NT // 2 - 1) as i:
                if own:
                    own.start(i - 3, steps)
                body(i, 0, Parts())
                body(i, 1, Parts())
            if own:
                own.end(NT // 2 - 4)
            for j in range(NT - 2, NT + 3):
                body(j // 2, j % 2, Parts(j))

        @block.sync
        def _(sp):
            def load_w(k):
                src = t["a_mat"] if k < KT else t["b_mat"]
                sp.dma_start(raw[:, k % RAW], src[(k % KT) * P:(k % KT + 1) * P]).then_inc(ld_w[k % RAW], 16)

            def load_xa(j, s):
                sp.dma_start(xa[:, s], tiles("x1")[j]).then_inc(ld_xa[s], 16)

            load_xa(0, 0)
            for k in range(RAW):
                load_w(k)
            load_xa(1, 1)
            sp.dma_start(gain[:], rows_all(t["g_xattn_post"])).then_inc(ld_const, 16)
            sp.dma_start(g_ffn[:], t["g_ffn_pre_cols"]).then_inc(ld_const, 16)

            def load_ws(ks):
                for k in ks:
                    sp.wait_ge(w_lo_ready, k - RAW + 1)
                    load_w(k)

            load_ws(range(RAW, KT + RAW))

            def body(h, s, p):
                j = 2 * h + s
                if p.post:
                    sp.wait_ge(x2_ready, j - 2)
                    sp.dma_start(tiles("x2")[j - 3], x2[:, 1 - s]).then_inc(stored[1 - s], 16)
                if p.out:
                    if p.j == 2:
                        sp.wait_ge(w_lo_ready, 2 * KT)
                    sp.dma_start(xb, tiles("x1")[j - 2]).then_inc(ld_xb, 16)
                if p.ahead2:
                    sp.wait_ge(h_ready, j + 1)
                    load_xa(j + 2, s)
                if p.j in (0, 1):
                    load_ws(range(KT + RAW + 4 * p.j, min(KT + RAW + 4 + 4 * p.j, 2 * KT)))
                if p.post:
                    sp.wait_ge(h3_t_ready, j - 2)
                    sp.dma_start(t["h3_t"][:, :, bass.ds((j - 3) * P, P)].rearrange("k p l -> p k l"),
                                 h3_t[:]).then_inc(stored3, 16)

            turns(sp, body)
            for s in range(2):
                sp.wait_ge(stored[s], 16 * (NT // 2))
            sp.wait_ge(stored3, 16 * NT)

        @block.scalar
        def _(act):
            own = act_own.of(act)
            act.preload_act_table_set(LOG_EXP)

            def split(k):
                act.wait_ge(ld_w[k % RAW], 16 * (k // RAW + 1))
                nc.scalar.activation((a_hi if k < KT else b_hi)[:, k % KT], raw[:, k % RAW],
                                     ACT.Copy).then_inc(w_hi_ready, 1)

            def stats(h, s):
                j = 2 * h + s
                act.wait_ge(ld_xa[s], 16 * (h + 1))
                if not (isinstance(j, int) and j == 0):
                    act.wait_ge(h_ready, j)
                own.after(nc.scalar.activation(junk[:], xa[:, s], ACT.Square, accum_out=x_st[0][:]))
                rsqrt_start(nc, own, x_st[1][:], x_st[0][:], 1.0 / D, EPS).then_inc(x_guess, 1)

            def high_h(j, s):
                act.wait_ge(h_turned, j + 1)
                nc.scalar.activation(h_hi[:, s], tr[:], ACT.Copy).then_inc(h_hi_ready, 1)

            stats(0, 0)
            split(0)
            high_h(0, 0)
            for k in range(1, KT):
                split(k)
                if k == 4:
                    stats(0, 1)

            def high_p(j, s):
                act.wait_ge(p_turned, j)
                nc.scalar.activation(p_hi[:, 1 - s], tr[:], ACT.Copy).then_inc(p_hi_ready, 1)

            def body(h, s, p):
                j = 2 * h + s
                if p.probs and not p.scores:
                    high_p(j, s)
                if p.post:
                    act.wait_ge(y_done, j - 2)
                    own.after(nc.scalar.activation(junk[:], flat(out_ps(p)), ACT.Square, accum_out=y_st[0][:]))
                    rsqrt_start(nc, own, y_st[1][:], y_st[0][:], 1.0 / D, EPS).then_inc(y_guess, 1)
                    act.wait_ge(x2_ready, j - 2)
                    own.after(nc.scalar.activation(junk[:], x2[:, 1 - s], ACT.Square, accum_out=z_st[0][:]))
                    rsqrt_start(nc, own, z_st[1][:], z_st[0][:], 1.0 / D, EPS).then_inc(z_guess, 1)
                if p.ahead:
                    high_h(j + 1, 1 - s)
                if p.ahead2:
                    stats(h + 1, s)
                if p.probs and p.scores:
                    high_p(j, s)
                if p.scores:
                    act.wait_ge(max_ready, j + 1)
                    for hd in range(HEADS):
                        at = slice(hd * N_MEM, (hd + 1) * N_MEM)
                        ins = nc.scalar.activation(probs[:, at], flat(s_ps)[:, at], ACT.Exp,
                                                   bias=neg_max[:, hd:hd + 1], accum_out=sums[:, hd:hd + 1])
                    ins.then_inc(exps, 1)
                if p.j in (0, 1):
                    for k in range(KT + 4 * p.j, KT + 4 * p.j + 4):
                        split(k)

            turns(act, body, own, 12)

        @block.vector
        def _(dve):
            own = dve_own.of(dve)

            def split(k):
                dve.wait_ge(w_hi_ready, k + 1)
                hi, lo = (a_hi, a_lo) if k < KT else (b_hi, b_lo)
                nc.vector.tensor_tensor(lo[:, k % KT], raw[:, k % RAW], hi[:, k % KT].bitcast(F32),
                                        ALU.subtract).then_inc(w_lo_ready, 1)

            def normalise(j, s):
                dve.wait_ge(x_guess, j + 1)
                own.after(rsqrt_end(nc, own, x_st[3][:], x_st[1][:], x_st[0][:], x_st[2][:], 1.0 / D, EPS))
                if not (isinstance(j, int) and j == 0):
                    dve.wait_ge(h_turned, j)
                nc.vector.tensor_scalar(h_buffer[:], xa[:, s], x_st[3][:], None, ALU.mult).then_inc(h_ready, 1)

            def low_h(j, s):
                dve.wait_ge(h_hi_ready, j + 1)
                nc.vector.tensor_tensor(h_lo[:, s], tr[:], h_hi[:, s].bitcast(F32), ALU.subtract).then_inc(h_lo_ready, 1)

            normalise(0, 0)
            split(0)
            low_h(0, 0)
            for k in range(1, KT):
                split(k)
                if k == 5:
                    normalise(1, 1)
            dve.wait_ge(ld_const, 32)

            def low_p(j, s):
                dve.wait_ge(p_hi_ready, j)
                nc.vector.tensor_tensor(p_lo[:, 1 - s], tr[:], p_hi[:, 1 - s].bitcast(F32),
                                        ALU.subtract).then_inc(p_lo_ready, 1)

            def body(h, s, p):
                j = 2 * h + s
                if p.ahead and p.j != 0:
                    normalise(j + 1, 1 - s)
                if p.probs and not p.scores:
                    low_p(j, s)
                if p.post:
                    dve.wait_ge(y_guess, j - 2)
                    own.after(rsqrt_end(nc, own, y_st[3][:], y_st[1][:], y_st[0][:], y_st[2][:], 1.0 / D, EPS))
                    at_least(dve, stored[1 - s], 16 * (h - 1 if s else h - 2))
                    own.after(nc.vector.scalar_tensor_tensor(x2[:, 1 - s], flat(out_ps(p)), y_st[3][:], gain[:], ALU.mult,
                                                             ALU.mult))
                    dve.wait_ge(ld_xb, 16 * (j - 2))
                    nc.vector.tensor_tensor(x2[:, 1 - s], x2[:, 1 - s], xb, ALU.add).then_inc(x2_ready, 1)
                    dve.wait_ge(z_guess, j - 2)
                    own.after(rsqrt_end(nc, own, z_st[3][:], z_st[1][:], z_st[0][:], z_st[2][:], 1.0 / D, EPS))
                    if p.j != 3:
                        dve.wait_ge(x_turned, j - 3)
                    nc.vector.tensor_scalar(h3, x2[:, 1 - s], z_st[3][:], None, ALU.mult).then_inc(h3_ready, 1)
                if p.ahead:
                    low_h(j + 1, 1 - s)
                if p.scores:
                    dve.wait_ge(s_done, j + 1)
                    if p.j != 0:
                        dve.wait_ge(exps, j)
                    own.after(nc.vector.tensor_reduce(neg_max[:], by_head(flat(s_ps)), AX_X, ALU.max))
                    nc.vector.tensor_scalar(neg_max[:], neg_max[:], -1.0, None, ALU.mult).then_inc(max_ready, 1)
                if p.post:
                    dve.wait_ge(x_turned, j - 2)
                    if p.j != 3:
                        dve.wait_ge(stored3, 16 * (j - 3))
                    nc.vector.tensor_tensor(h3_t[:], tr3[:], g_ffn[:].unsqueeze(2).to_broadcast([P, KT, P]),
                                            ALU.mult).then_inc(h3_t_ready, 1)
                if p.probs and p.scores:
                    low_p(j, s)
                if p.scores:
                    dve.wait_ge(exps, j + 1)
                    own.after(nc.vector.reciprocal(sums[:], sums[:]))
                    nc.vector.tensor_tensor(by_head(probs[:]), by_head(probs[:]),
                                            sums[:].unsqueeze(2).to_broadcast([P, HEADS, N_MEM]),
                                            ALU.mult).then_inc(probs_ready, 1)
                if p.j in (0, 1):
                    for k in range(KT + 4 * p.j, KT + 4 * p.j + 4):
                        split(k)

            turns(dve, body, own, 36)

        @block.tensor
        def _(pe):
            def turn_h(j, s):
                pe.wait_ge(h_ready, j + 1)
                if not (isinstance(j, int) and j < 3):
                    pe.wait_ge(p_lo_ready, j - 2)
                for k in range(KT):
                    ins = nc.tensor.transpose(tr[:, k], h_buffer[:, k * P:(k + 1) * P], ident[:])
                ins.then_inc(h_turned, 1)

            def product_k(out, hi, lo, w_hi, w_lo, n, k):
                nc.tensor.matmul(out, hi[:, k], w_hi[:, k, n], start=(k == 0), stop=False)
                nc.tensor.matmul(out, hi[:, k], w_lo[:, k, n], start=False, stop=False)
                return nc.tensor.matmul(out, lo[:, k], w_hi[:, k, n], start=False, stop=(k == KT - 1))

            def product(*what):
                for k in range(KT):
                    ins = product_k(*what, k)
                return ins

            def turn_x(p, j):
                pe.wait_ge(h3_ready, j - 2)
                if p.j != 3:
                    pe.wait_ge(h3_t_ready, j - 3)
                for k in range(KT):
                    ins = nc.tensor.transpose(tr3[:, k], h3[:, k * P:(k + 1) * P], ident[:])
                ins.then_inc(x_turned, 1)

            halves = [slice(half * BANK, (half + 1) * BANK) for half in range(2)]

            turn_h(0, 0)

            def body(h, s, p):
                j = 2 * h + s
                if p.scores:
                    pe.wait_ge(h_lo_ready, j + 1)
                    if p.j == 0:
                        for k in range(KT):
                            pe.wait_ge(w_lo_ready, k + 1)
                            for half in range(2):
                                ins = product_k(s_ps[:, half], h_hi[:, s], h_lo[:, s], a_hi, a_lo, halves[half], k)
                        ins.then_inc(s_done, 1)
                        turn_h(1, 1)
                    else:
                        pe.wait_ge(exps, j)
                        product(s_ps[:, 0], h_hi[:, s], h_lo[:, s], a_hi, a_lo, halves[0])
                        if p.ahead:
                            turn_h(j + 1, 1 - s)
                        product(s_ps[:, 1], h_hi[:, s], h_lo[:, s], a_hi, a_lo, halves[1]).then_inc(s_done, 1)
                if p.post and p.scores:
                    turn_x(p, j)
                if p.probs:
                    pe.wait_ge(probs_ready, j)
                    if p.ahead:
                        pe.wait_ge(h_lo_ready, j + 2)
                    for k in range(KT):
                        ins = nc.tensor.transpose(tr[:, k], probs[:, k * P:(k + 1) * P], ident[:])
                    ins.then_inc(p_turned, 1)
                if p.out:
                    pe.wait_ge(p_lo_ready, j - 1)
                    pe.wait_ge(w_lo_ready, 2 * KT)
                    to = y_ps
                    if p.j == NT:
                        to = s_ps
                        pe.wait_ge(exps, NT)
                    elif p.post:
                        pe.wait_ge(x2_ready, j - 3 if p.j == NT + 1 else j - 2)
                    for half in range(2):
                        ins = product(to[:, half], p_hi[:, s], p_lo[:, s], b_hi, b_lo, halves[half])
                    ins.then_inc(y_done, 1)
                if p.post and not p.scores:
                    turn_x(p, j)

            turns(pe, body)

def ffn(nc, t, act_own, dve_own):
    with Scope(nc, "ff") as c:
        BLOCKS = 2
        TB = SEQ // BLOCKS
        TT = TB // P
        CHUNKS = D_FF // (2 * P)
        RING = 4
        FIRST = 4
        TURN = 6
        opening = [("gu", 0), ("h", 0), ("gu", 1)] + [("h", k) for k in range(1, KT)] + [("gu", 2), ("gu", 3)]
        turn_base = [KT + FIRST]
        h_base = [0, turn_base[0] + TURN * CHUNKS]
        x_base = [h_base[1] + KT]
        turn_base.append(x_base[0] + TT)
        x_base.append(turn_base[1] + TURN * CHUNKS - FIRST)

        raw = c.sb("raw", [P, RING, D])
        h_hi, h_lo = c.sb("h_hi", [P, KT, TB], FR), c.sb("h_lo", [P, KT, TB], FR)
        gu_hi, gu_lo = c.sb("gu_hi", [P, 4, KT, P], FR), c.sb("gu_lo", [P, 4, KT, P], FR)
        wd_hi, wd_lo = c.sb("wd_hi", [P, 2, D], FR), c.sb("wd_lo", [P, 2, D], FR)
        act_hi, act_lo = c.sb("act_hi", [P, 2, 2, TB], FR), c.sb("act_lo", [P, 2, 2, TB], FR)
        y = c.sb("y", [P, TT, D])
        silu, hidden = c.sb("silu", [P, 2, BANK]), c.sb("hidden", [P, 2, BANK])
        gain = c.sb("gain", [P, D])
        ss, y0, tmp, rs = (c.sb(n, [P, TT]) for n in ("ss", "y0", "tmp", "rs"))
        gate_ps, up_ps, down_ps = c.ps("gate", [P, 2, BANK]), c.ps("up", [P, 2, BANK]), c.ps("down", [P, 4, BANK])
        ld, ld_gain = c.sems("ld", RING), c.sem("ld_gain")
        hi_ready, lo_ready, gate_done, up_done, down_done = (
            c.sem(n) for n in ("hi_ready", "lo_ready", "gate_done", "up_done", "down_done"))
        silu_ready, hidden_ready, act_hi_ready, act_ready, added, guess, stored = (
            c.sem(n) for n in ("silu_ready", "hidden_ready", "act_hi_ready", "act_ready", "added", "guess", "stored"))
        gained = c.sem("gained")
        flat4 = lambda ap: ap.rearrange("p k n -> p (k n)")
        block = c.enter_context(nc.Block())
        y_gain = [flat4(silu[:]), flat4(hidden[:])]
        GROUPS = 2 * TT
        x2_d = t["x2"].rearrange("(t p) d -> t p d", p=P)
        out_d = t["out"].rearrange("(t p) d -> t p d", p=P)

        class Num:

            def __init__(self, base, i=0):
                self.base, self.i, self.slot = base, i, base % RING
                self.count = base + 12 * i + 1
                self.loads = base // RING + 1 + 3 * i
                self.first = isinstance(i, int) and base + 12 * i < RING

        def turns(eng, body, b, own=None, steps=0):
            body(0, 0, True, False)
            body(0, 1, True, True)
            with eng.Fori(1, CHUNKS // 2) as i:
                if own:
                    own.start(i - 1, steps)
                body(i, 0, True, True)
                body(i, 1, True, True)
            if own:
                own.end(CHUNKS // 2 - 1)
            body(CHUNKS // 2, 0, True, True)
            body(CHUNKS // 2, 1, False, True)

        def last_turn(i, e):
            return isinstance(i, int) and 2 * i + e == CHUNKS - 1

        def down_weights(b, c):
            if b == BLOCKS - 1 and isinstance(c, int) and c == CHUNKS - 1:
                return [flat4(gu_hi[:, q]) for q in range(2)], [flat4(gu_lo[:, q]) for q in range(2)]
            return [wd_hi[:, q] for q in range(2)], [wd_lo[:, q] for q in range(2)]

        def ring_turn(b, i, e):
            base = turn_base[b] + TURN * e
            gate_up = [] if b == BLOCKS - 1 and last_turn(i, e) else [Num(base + q, i) for q in range(4)]
            downs = [Num(base + len(gate_up) + q, i) for q in range(2)]
            return gate_up, downs

        @block.sync
        def _(sp):
            def load(n, src):
                if not n.first:
                    sp.wait_ge(lo_ready, n.count - RING)
                sp.dma_start(raw[:, n.slot], src).then_inc(ld[n.slot], 16)

            def load_gate_up(n, q, chunk):
                name, tile = ("w_gate", "w_up")[q % 2], 2 * chunk + q // 2
                load(n, t[name][tile].rearrange("p k n -> p (k n)"))

            def load_h(b):
                for k in range(KT):
                    load(Num(h_base[b] + k), t["h3_t"][k, :, b * TB:(b + 1) * TB])

            for n, (kind, at) in enumerate(opening):
                if kind == "h":
                    load(Num(n), t["h3_t"][at, :, 0:TB])
                else:
                    load_gate_up(Num(n), at, 0)
            sp.dma_start(gain[:], rows_all(t["g_ffn_post"])).then_inc(ld_gain, 16)
            for b in range(BLOCKS):
                def body(i, e, gates, downs):
                    if not gates:
                        return
                    chunk = 2 * i + e
                    following = 0 if last_turn(i, e) else chunk + 1
                    gate_up, down = ring_turn(b, i, e)
                    for q, n in enumerate(gate_up):
                        load_gate_up(n, q, following)
                    for q, n in enumerate(down):
                        load(n, t["w_down"][bass.ds((2 * chunk + q) * P, P)])

                turns(sp, body, b)
                if b + 1 < BLOCKS:
                    load_h(b + 1)
                for i in range(TT):
                    load(Num(x_base[b] + i), x2_d[b * TT + i])
                for i in range(TT):
                    sp.wait_ge(lo_ready, Num(x_base[b] + i).count)
                    sp.dma_start(out_d[b * TT + i], y[:, i]).then_inc(stored, 16)
            sp.wait_ge(stored, 16 * NT)

        def split_hi(act, n, to, b):
            act.wait_ge(ld[n.slot], 16 * n.loads)
            nc.scalar.activation(to, raw[:, n.slot], ACT.Copy).then_inc(hi_ready, 1)

        def split_lo(dve, n, to, hi, b):
            dve.wait_ge(hi_ready, n.count - TT * b)
            nc.vector.tensor_tensor(to, raw[:, n.slot], hi.bitcast(F32), ALU.subtract).then_inc(lo_ready, 1)

        @block.gpsimd
        def _(g):
            b = BLOCKS - 1
            g.wait_ge(ld_gain, 16)
            for i in range(TT):
                g.wait_ge(added, GROUPS * (CHUNKS * BLOCKS - 1) + 2 * i + 2)
                if i >= 2:
                    g.wait_ge(lo_ready, Num(x_base[b] + i - 2).count)
                nc.gpsimd.tensor_tensor(y_gain[i % 2], y[:, i], gain[:], ALU.mult).then_inc(gained, 1)

        @block.scalar
        def _(act):
            own = act_own.of(act)
            act.preload_act_table(ACT.Silu)
            for n, (kind, at) in enumerate(opening):
                split_hi(act, Num(n), h_hi[:, at] if kind == "h" else flat4(gu_hi[:, at]), 0)
            for b in range(BLOCKS):
                def body(i, e, gates, downs):
                    g = CHUNKS * b + 2 * i + e
                    if not gates:
                        if b + 1 < BLOCKS:
                            for k in range(KT):
                                split_hi(act, Num(h_base[b + 1] + k), h_hi[:, k], b)
                        act.preload_act_table_set(LOG_EXP)
                        for i in range(TT):
                            act.wait_ge(added, GROUPS * (CHUNKS * (b + 1) - 1) + 2 * i + 2)
                            unread = flat4(gate_ps[:]) if b + 1 == BLOCKS else flat4(silu[:])
                            own.after(nc.scalar.activation(unread, y[:, i], ACT.Square, accum_out=ss[:, i:i + 1]))
                            col = slice(i, i + 1)
                            ins = rsqrt_start(nc, own, y0[:, col], ss[:, col], 1.0 / D, EPS)
                            if b + 1 == BLOCKS:
                                own.after(ins)
                                ins = rsqrt_end_act(nc, own, rs[:, col], y0[:, col], ss[:, col], tmp[:, col], 1.0 / D,
                                                    EPS)
                            ins.then_inc(guess, 1)
                        if b + 1 < BLOCKS:
                            act.preload_act_table(ACT.Silu)
                        return
                    gate_up, down = ring_turn(b, i, e)
                    for tile in range(2):
                        for half in range(2):
                            m = 4 * g + 2 * tile + half
                            early = isinstance(i, int) and b == 0 and i == 0 and e == 0 and tile == 0
                            act.wait_ge(gate_done, m + 1)
                            if not early:
                                at_least(act, hidden_ready, m - 1)
                            nc.scalar.activation(silu[:, half], gate_ps[:, half], ACT.Silu).then_inc(silu_ready, 1)
                            act.wait_ge(hidden_ready, m + 1)
                            if downs or b:
                                at_least(act, down_done, GROUPS * (g - 1))
                            nc.scalar.activation(act_hi[:, e, tile, half * BANK:(half + 1) * BANK], hidden[:, half],
                                                 ACT.Copy).then_inc(act_hi_ready, 1)
                        for q in (2 * tile, 2 * tile + 1):
                            if gate_up:
                                act.wait_ge(up_done, 4 * g + 2 * tile + 2)
                                split_hi(act, gate_up[q], flat4(gu_hi[:, q]), b)
                    if b == BLOCKS - 1 and last_turn(i, e):
                        act.wait_ge(up_done, 4 * g + 2)
                    elif downs or b:
                        act.wait_ge(down_done, GROUPS * g)
                    w_hi, w_lo = down_weights(b, 2 * i + e)
                    for q in range(2):
                        split_hi(act, down[q], w_hi[q], b)

                turns(act, body, b)

        @block.vector
        def _(dve):
            own = dve_own.of(dve)
            for n, (kind, at) in enumerate(opening):
                if kind == "h":
                    split_lo(dve, Num(n), h_lo[:, at], h_hi[:, at], 0)
                else:
                    split_lo(dve, Num(n), flat4(gu_lo[:, at]), flat4(gu_hi[:, at]), 0)
            dve.wait_ge(ld_gain, 16)
            for b in range(BLOCKS):
                def add(g, r, first):
                    dve.wait_ge(down_done, GROUPS * (g - 1) + r + 1)
                    to = y[:, r // 2, (r % 2) * BANK:(r % 2 + 1) * BANK]
                    if first:
                        if b:
                            dve.wait_ge(stored, 16 * TT * b)
                        nc.vector.tensor_copy(to, down_ps[:, r % 4]).then_inc(added, 1)
                    else:
                        nc.vector.tensor_tensor(to, down_ps[:, r % 4], to, ALU.add).then_inc(added, 1)

                def finish(i):
                    n, col = Num(x_base[b] + i), slice(i, i + 1)
                    if b + 1 == BLOCKS:
                        dve.wait_ge(gained, i + 1)
                        dve.wait_ge(guess, TT * b + i + 1)
                        dve.wait_ge(ld[n.slot], 16 * n.loads)
                        nc.vector.scalar_tensor_tensor(y[:, i], y_gain[i % 2], rs[:, col], raw[:, n.slot], ALU.mult,
                                                       ALU.add).then_inc(lo_ready, 1)
                        return
                    dve.wait_ge(guess, TT * b + i + 1)
                    own.after(rsqrt_end(nc, own, rs[:, col], y0[:, col], ss[:, col], tmp[:, col], 1.0 / D, EPS))
                    own.after(nc.vector.scalar_tensor_tensor(y[:, i], y[:, i], rs[:, col], gain[:], ALU.mult,
                                                             ALU.mult))
                    dve.wait_ge(ld[n.slot], 16 * n.loads)
                    nc.vector.tensor_tensor(y[:, i], y[:, i], raw[:, n.slot], ALU.add).then_inc(lo_ready, 1)

                def body(i, e, gates, downs):
                    g = CHUNKS * b + 2 * i + e
                    first = isinstance(i, int) and i == 0
                    if not gates:
                        for r in range(GROUPS):
                            add(g, r, False)
                            if b + 1 < BLOCKS and r % 2:
                                k = r // 2
                                split_lo(dve, Num(h_base[b + 1] + k), h_lo[:, k], h_hi[:, k], b)
                            if b + 1 == BLOCKS and r % 2 and r // 2 >= 2:
                                finish(r // 2 - 2)
                        for i in range(TT - 2 if b + 1 == BLOCKS else 0, TT):
                            finish(i)
                        return
                    gate_up, down = ring_turn(b, i, e)
                    for tile in range(2):
                        for half in range(2):
                            m = 4 * g + 2 * tile + half
                            at = (slice(None), e, tile, slice(half * BANK, (half + 1) * BANK))
                            dve.wait_ge(silu_ready, m + 1)
                            dve.wait_ge(up_done, m + 1)
                            nc.vector.tensor_tensor(hidden[:, half], up_ps[:, half], silu[:, half],
                                                    ALU.mult).then_inc(hidden_ready, 1)
                            dve.wait_ge(act_hi_ready, m + 1)
                            dve.wait_ge(hidden_ready, m + 1)
                            nc.vector.tensor_tensor(act_lo[at], hidden[:, half], act_hi[at].bitcast(F32),
                                                    ALU.subtract).then_inc(act_ready, 1)
                        for q in (2 * tile, 2 * tile + 1):
                            if gate_up:
                                split_lo(dve, gate_up[q], flat4(gu_lo[:, q]), flat4(gu_hi[:, q]), b)
                    def low_down():
                        w_hi, w_lo = down_weights(b, 2 * i + e)
                        for q in range(2):
                            split_lo(dve, down[q], w_lo[q], w_hi[q], b)

                    last = b == BLOCKS - 1 and last_turn(i, e)
                    if last:
                        low_down()
                    if downs:
                        for r in range(GROUPS):
                            if not first:
                                dve.wait_ge(added, GROUPS * (g - 2) + r + 1)
                            add(g, r, first)
                    if not last:
                        low_down()

                turns(dve, body, b)

        @block.tensor
        def _(pe):
            def gate_up_k(ps, q, k, half):
                tok = slice(half * BANK, (half + 1) * BANK)
                nc.tensor.matmul(ps[:, half], gu_hi[:, q, k], h_hi[:, k, tok], start=(k == 0), stop=False)
                nc.tensor.matmul(ps[:, half], gu_hi[:, q, k], h_lo[:, k, tok], start=False, stop=False)
                return nc.tensor.matmul(ps[:, half], gu_lo[:, q, k], h_hi[:, k, tok], start=False,
                                        stop=(k == KT - 1))

            for b in range(BLOCKS):
                def body(i, e, gates, downs):
                    g = CHUNKS * b + 2 * i + e
                    start = isinstance(i, int) and b == 0 and i == 0 and e == 0
                    if gates:
                        for tile in range(2):
                            if start:
                                if tile:
                                    pe.wait_ge(lo_ready, len(opening))
                            elif isinstance(i, int) and i == 0 and e == 0:
                                n = Num(turn_base[0] + TURN * (CHUNKS - 1) + 2 * tile + 1)
                                pe.wait_ge(lo_ready, n.count)
                                pe.wait_ge(lo_ready, h_base[b] + KT)
                            else:
                                base = turn_base[b] + (0 if e else TURN - 12)
                                pe.wait_ge(lo_ready, Num(base + 2 * tile + 1, i).count)
                            if start and tile == 0:
                                for k in range(KT):
                                    pe.wait_ge(lo_ready, opening.index(("h", k)) + 1)
                                    for ps, q, done in ((gate_ps, 0, gate_done), (up_ps, 1, up_done)):
                                        pe.wait_ge(lo_ready, opening.index(("gu", q)) + 1)
                                        for half in range(2):
                                            ins = gate_up_k(ps, q, k, half)
                                            if k == KT - 1:
                                                ins.then_inc(done, 1)
                                continue
                            for half in range(2):
                                m = 4 * g + 2 * tile + half
                                for ps, q, done, read in ((gate_ps, 2 * tile, gate_done, silu_ready),
                                                          (up_ps, 2 * tile + 1, up_done, hidden_ready)):
                                    pe.wait_ge(read, m - 1)
                                    for k in range(KT):
                                        ins = gate_up_k(ps, q, k, half)
                                    ins.then_inc(done, 1)
                    if downs:
                        base = turn_base[b] + (0 if e else -TURN) + 5
                        short = b == BLOCKS - 1 and not gates
                        pe.wait_ge(lo_ready, Num(base - (4 if short else 0), i).count)
                        pe.wait_ge(act_ready, 4 * g)
                        w_hi, w_lo = down_weights(b, 2 * i + e - 1)
                        for r in range(GROUPS):
                            tok, n = slice((r // 2) * P, (r // 2 + 1) * P), slice((r % 2) * BANK, (r % 2 + 1) * BANK)
                            if not (isinstance(i, int) and b == 0 and i == 0 and r < 4):
                                pe.wait_ge(added, GROUPS * (g - 1) + r - 3)
                            for tile in range(2):
                                w = (w_hi[tile][:, n], w_lo[tile][:, n])
                                a_hi, a_lo = act_hi[:, 1 - e, tile, tok], act_lo[:, 1 - e, tile, tok]
                                nc.tensor.matmul(down_ps[:, r % 4], a_hi, w[0], start=(tile == 0), stop=False)
                                nc.tensor.matmul(down_ps[:, r % 4], a_hi, w[1], start=False, stop=False)
                                ins = nc.tensor.matmul(down_ps[:, r % 4], a_lo, w[0], start=False, stop=(tile == 1))
                            ins.then_inc(down_done, 1)

                turns(pe, body, b)

SCRATCH = {
    "a_mat": (D, D), "b_mat": (D, D), "pool_out": (4 * P, D),
    "proj": (PANELS, P, SEQ), "gate_rows": (4 * HEADS, SEQ), "chunk_ends": (HC, 2), "m_prev": (HEADS, NT),
    "neg_m": (HEADS, SEQ), "inter": (HEADS, SEQ), "decay": (HC,),
    "x1": (SEQ, D), "x2": (SEQ, D), "h3_t": (KT, P, SEQ),
}


def program(nc, t):
    Scope.taken.clear()
    with Scope(nc, "all") as c:
        ident = c.sb("ident", [P, P])
        own = Order(c.sem("act_own")), Order(c.sem("dve_own"))
        with Scope(nc, "mix") as mc:
            gate_rows = [mc.sb(n, [HC, P]) for n in ("gate_a", "gate_wk", "gate_en")]
            with Scope(nc, "h") as hc:
                h_hi, h_lo = hc.sb("hi", [P, KT, SEQ], FR), hc.sb("lo", [P, KT, SEQ], FR)
                fold_and_norm(nc, t, *own, ident, h_hi, h_lo)
                mix_in(nc, t, *own, h_hi, h_lo, gate_rows)
            mlstm_out(nc, t, *own, ident, gate_rows)
        cross(nc, t, *own, ident)
        ffn(nc, t, *own)


def laid_out(i):
    import numpy as np

    f = lambda name: np.ascontiguousarray(i[name])[0]
    ins = {n: f(n) for n in (
        "x", "mem", "b_gate", "w_out", "g_mix_pre", "g_mix_post", "g_xattn_post", "g_ffn_post")}
    for name in ("g_mem", "g_xattn_pre", "pool_scale", "mlstm_norm_g", "g_ffn_pre"):
        ins[name + "_cols"] = f(name).reshape(-1, P).T
    panels = lambda w, n: w.reshape(KT, P, n, P).transpose(2, 1, 0, 3)
    ins["wk"], ins["wv"], ins["wo"] = panels(f("wk_x"), KT), panels(f("wv_x"), KT), f("wo_x")
    ins["wqt"] = panels(f("wq_x").T, KT)
    ins["w_pool_t"] = f("w_pool").transpose(0, 2, 1)
    w_in = f("w_in")
    gates = np.zeros((D, P), w_in.dtype)
    for j in range(4):
        at = 5 * BANK + (j % 2) * HEADS
        gates[:, 32 * j:32 * j + HEADS] = w_in[:, at:at + HEADS]
    cols = lambda n: w_in[:, n * BANK:(n + 1) * BANK]
    w = np.concatenate([gates, cols(1), cols(2), cols(0), cols(4), cols(3)], axis=1)
    ins["w_in"] = panels(w, PANELS)
    conv = f("conv_qk")
    ins["conv"] = conv.reshape(4, KT, P).transpose(2, 1, 0)
    for name in ("w_gate", "w_up"):
        ins[name] = panels(f(name), D_FF // P)
    ins["w_down"] = f("w_down")
    return {k: np.ascontiguousarray(v) for k, v in ins.items()}


def kernel(**inputs):
    import numpy as np
    import concourse.bacc as bacc
    from concourse.bass_utils import run_bass_kernel_spmd

    nc = bacc.Bacc("TRN2", target_bir_lowering=False, num_devices=1)
    ins = laid_out(inputs)
    t = {k: nc.dram_tensor(f"in_{k}", v.shape, mybir.dt.from_np(v.dtype), kind="ExternalInput").ap()
         for k, v in ins.items()}
    for k, shape in SCRATCH.items():
        t[k] = nc.dram_tensor(f"scratch_{k}", shape, F32, kind="Internal").ap()
    t["out"] = nc.dram_tensor("out", (SEQ, D), F32, kind="ExternalOutput").ap()
    program(nc, t)
    r = run_bass_kernel_spmd(nc, [{f"in_{k}": v for k, v in ins.items()}], core_ids=[0])
    return r.results[0]["out"].reshape(1, SEQ, D)
```
